# Optimizing a Trainium2 kernel written in Bass

```python
import math
import jax, jax.numpy as jnp
from jax import lax
import numpy as np

D_MODEL = 1024
BATCH = 1
SEQ = 256
DEPTH = 2

RET_HEADS = 4
RET_DK = 128
RET_DV = 128
RET_CHUNK = 128
ROPE_BASE = 10000.0
NSA_HEADS = 8
NSA_KV_GROUPS = 2
NSA_HPG = NSA_HEADS // NSA_KV_GROUPS
NSA_HD = 64
CMP_BLOCK = 32
CMP_STRIDE = 16
SLC_BLOCK = 64
N_SELECT = 8
FORCED_LOCAL = 2
FORCE_BONUS = 1.0e4
WINDOW = 512
Q_BLOCK = 128
HGRN_HEADS = 8
HGRN_DK = D_MODEL // HGRN_HEADS
HGRN_DV = D_MODEL // HGRN_HEADS
HGRN_CHUNK = 64
D_FF = -(-8 * D_MODEL // (3 * 256)) * 256
EPS = 1e-6

EVEN_SIZES = ([RET_HEADS * RET_DK] * 2 + [RET_HEADS * RET_DV] * 2 + [NSA_HEADS * NSA_HD]
              + [NSA_KV_GROUPS * NSA_HD] * 6 + [3 * NSA_HEADS])
EVEN_IN = sum(EVEN_SIZES)
EVEN_MIX = RET_HEADS * RET_DV + NSA_HEADS * NSA_HD
ODD_SIZES = [HGRN_HEADS * HGRN_DK] * 2 + [HGRN_HEADS * HGRN_DV] * 2
ODD_IN = sum(ODD_SIZES)
ODD_MIX = HGRN_HEADS * HGRN_DV
N_EVEN = (DEPTH + 1) // 2
N_ODD = DEPTH // 2


def _split(a, sizes):
    return jnp.split(a, list(np.cumsum(sizes)[:-1]), axis=-1)

def rmsnorm(x, g):
    xf = x.astype(jnp.float32)
    y = xf * lax.rsqrt(jnp.mean(xf * xf, axis=-1, keepdims=True) + EPS)
    return (y * g.astype(jnp.float32)).astype(x.dtype)

def rotary(x):
    S, d = x.shape[-2], x.shape[-1]
    half = d // 2
    inv = ROPE_BASE ** (-jnp.arange(half, dtype=jnp.float32) / half)
    ang = jnp.arange(S, dtype=jnp.float32)[:, None] * inv[None, :]
    cos, sin = jnp.cos(ang), jnp.sin(ang)
    x1, x2 = x[..., :half], x[..., half:]
    return jnp.concatenate([x1 * cos - x2 * sin, x1 * sin + x2 * cos], axis=-1)

def masked_softmax(s, mask):
    s = jnp.where(mask, s, -jnp.inf)
    m = jnp.max(s, axis=-1, keepdims=True)
    m = jnp.where(jnp.isfinite(m), m, 0.0)
    p = jnp.exp(s - m)
    return p / jnp.maximum(jnp.sum(p, axis=-1, keepdims=True), 1e-30)

def retention_chunkwise(q, k, v):
    B, H, S, dk = q.shape
    dv = v.shape[-1]
    C = min(RET_CHUNK, S)
    NC = S // C
    log_gamma = jnp.log(1.0 - 2.0 ** (-5.0 - jnp.arange(H, dtype=jnp.float32)))
    q = q.reshape(B, H, NC, C, dk)
    k = k.reshape(B, H, NC, C, dk)
    v = v.reshape(B, H, NC, C, dv)
    idx = jnp.arange(C, dtype=jnp.float32)
    diff = idx[:, None] - idx[None, :]
    causal = diff >= 0
    dmat = jnp.where(causal, jnp.exp(log_gamma[:, None, None] * jnp.where(causal, diff, 0.0)), 0.0)
    scores = jnp.einsum('bhncd,bhnsd->bhncs', q, k) * dmat[None, :, None]
    o_inner = jnp.einsum('bhncs,bhnse->bhnce', scores, v)
    k_dec = k * jnp.exp(log_gamma[:, None] * (C - 1 - idx)[None, :])[None, :, None, :, None]
    chunk_kv = jnp.einsum('bhncd,bhnce->nbhde', k_dec, v)
    gamma_c = jnp.exp(log_gamma * C)[None, :, None, None]

    def step(state, kv):
        return gamma_c * state + kv, state

    _, r_prev = lax.scan(step, jnp.zeros((B, H, dk, dv), jnp.float32), chunk_kv)
    q_dec = q * jnp.exp(log_gamma[:, None] * (idx + 1.0)[None, :])[None, :, None, :, None]
    o_cross = jnp.einsum('bhncd,nbhde->bhnce', q_dec, r_prev)
    return (o_inner + o_cross).reshape(B, H, S, dv)

def nsa_compress(kv, pos_emb, w1, w2):
    B, G, S, d = kv.shape
    r = CMP_BLOCK // CMP_STRIDE
    parts = kv.reshape(B, G, S // CMP_STRIDE, CMP_STRIDE, d)
    n = S // CMP_STRIDE - r + 1
    blocks = jnp.concatenate([parts[:, :, j:j + n] for j in range(r)], axis=3)
    flat = (blocks + pos_emb.astype(jnp.float32)).reshape(B, G, n, CMP_BLOCK * d)
    return jax.nn.gelu(flat @ w1.astype(jnp.float32)) @ w2.astype(jnp.float32)

def nsa_attention(q, k_cmp, v_cmp, k_slc, v_slc, k_win, v_win, gates):
    B, G, HPG, S, d = q.shape
    scale = d ** -0.5
    n_cmp = k_cmp.shape[2]
    n_slc = S // SLC_BLOCK
    n_sel = min(N_SELECT, n_slc)
    cs = np.arange(n_cmp) * CMP_STRIDE
    ce = cs + CMP_BLOCK - 1
    ss = np.arange(n_slc) * SLC_BLOCK
    se = ss + SLC_BLOCK - 1
    overlap = jnp.asarray(((cs[:, None] <= se[None, :]) & (ce[:, None] >= ss[None, :])).astype(np.float32))
    cmp_end = jnp.asarray(ce.astype(np.int32))
    ks_blocks = k_slc.reshape(B, G, n_slc, SLC_BLOCK, d)
    vs_blocks = v_slc.reshape(B, G, n_slc, SLC_BLOCK, d)
    kw_pad = jnp.pad(k_win, ((0, 0), (0, 0), (WINDOW, 0), (0, 0)))
    vw_pad = jnp.pad(v_win, ((0, 0), (0, 0), (WINDOW, 0), (0, 0)))
    bi = jnp.arange(B)[:, None, None, None]
    gi = jnp.arange(G)[None, :, None, None]
    jblk = jnp.arange(n_slc)
    offs = jnp.arange(SLC_BLOCK)

    def block(i):
        q0 = i * Q_BLOCK
        t = q0 + jnp.arange(Q_BLOCK)
        qb = lax.dynamic_slice_in_dim(q, q0, Q_BLOCK, axis=3)
        s_c = jnp.einsum('bghqd,bgnd->bghqn', qb, k_cmp) * scale
        p_c = masked_softmax(s_c, cmp_end[None, :] <= t[:, None])
        o_c = jnp.einsum('bghqn,bgnd->bghqd', p_c, v_cmp)
        imp = jnp.einsum('bgqn,nj->bgqj', jnp.sum(p_c, axis=2), overlap)
        bt = (t // SLC_BLOCK)[:, None]
        valid_s = jblk[None, :] <= bt
        forced = (jblk[None, :] == 0) | ((bt - jblk[None, :] >= 0) & (bt - jblk[None, :] < FORCED_LOCAL))
        score = jnp.where(valid_s, imp + jnp.where(forced, FORCE_BONUS, 0.0), -1e30)
        _, idx = lax.top_k(score, n_sel)
        kg = ks_blocks[bi, gi, idx].reshape(B, G, Q_BLOCK, n_sel * SLC_BLOCK, d)
        vg = vs_blocks[bi, gi, idx].reshape(B, G, Q_BLOCK, n_sel * SLC_BLOCK, d)
        kpos = (idx[..., None] * SLC_BLOCK + offs).reshape(B, G, Q_BLOCK, n_sel * SLC_BLOCK)
        s_s = jnp.einsum('bghqd,bgqkd->bghqk', qb, kg) * scale
        p_s = masked_softmax(s_s, (kpos <= t[None, None, :, None])[:, :, None])
        o_s = jnp.einsum('bghqk,bgqkd->bghqd', p_s, vg)
        kw = lax.dynamic_slice_in_dim(kw_pad, q0, WINDOW + Q_BLOCK, axis=2)
        vw = lax.dynamic_slice_in_dim(vw_pad, q0, WINDOW + Q_BLOCK, axis=2)
        spos = q0 - WINDOW + jnp.arange(WINDOW + Q_BLOCK)
        dist = t[:, None] - spos[None, :]
        valid_w = (dist >= 0) & (dist < WINDOW) & (spos[None, :] >= 0)
        s_w = jnp.einsum('bghqd,bgkd->bghqk', qb, kw) * scale
        o_w = jnp.einsum('bghqk,bgkd->bghqd', masked_softmax(s_w, valid_w), vw)
        gb = lax.dynamic_slice_in_dim(gates, q0, Q_BLOCK, axis=4)[..., None]
        return gb[0] * o_c + gb[1] * o_s + gb[2] * o_w

    out = lax.map(block, jnp.arange(S // Q_BLOCK))
    return jnp.transpose(out, (1, 2, 3, 0, 4, 5)).reshape(B, G * HPG, S, d)

def retention_nsa_mixer(h, w_in, w_out, pos_k, w1_k, w2_k, pos_v, w1_v, w2_v):
    B, S, _ = h.shape
    proj = (h @ w_in).astype(jnp.float32)
    (rq, rk, rv, rg, nq, kc, vc, ks, vs, kw, vw, ng) = _split(proj, EVEN_SIZES)
    heads = lambda a, n: jnp.transpose(a.reshape(B, S, n, -1), (0, 2, 1, 3))
    q_r = rotary(heads(rq, RET_HEADS))
    k_r = rotary(heads(rk, RET_HEADS)) * RET_DK ** -0.5
    o_r = retention_chunkwise(q_r, k_r, heads(rv, RET_HEADS))
    mu = jnp.mean(o_r, axis=-1, keepdims=True)
    var = jnp.mean(jnp.square(o_r - mu), axis=-1, keepdims=True)
    o_r = (o_r - mu) * lax.rsqrt(var + 1e-5)
    o_r = jnp.transpose(o_r, (0, 2, 1, 3)).reshape(B, S, RET_HEADS * RET_DV) * jax.nn.silu(rg)
    q_n = jnp.transpose(nq.reshape(B, S, NSA_KV_GROUPS, NSA_HPG, NSA_HD), (0, 2, 3, 1, 4))
    kvh = lambda a: jnp.transpose(a.reshape(B, S, NSA_KV_GROUPS, NSA_HD), (0, 2, 1, 3))
    k_cmp = nsa_compress(kvh(kc), pos_k, w1_k, w2_k)
    v_cmp = nsa_compress(kvh(vc), pos_v, w1_v, w2_v)
    gates = jnp.transpose(jax.nn.sigmoid(ng).reshape(B, S, 3, NSA_KV_GROUPS, NSA_HPG), (2, 0, 3, 4, 1))
    o_n = nsa_attention(q_n, k_cmp, v_cmp, kvh(ks), kvh(vs), kvh(kw), kvh(vw), gates)
    o_n = jnp.transpose(o_n, (0, 2, 1, 3)).reshape(B, S, NSA_HEADS * NSA_HD)
    mixed = jnp.concatenate([o_r, o_n], axis=-1).astype(h.dtype)
    return mixed @ w_out

def hgrn2_chunkwise(q, k, v, log_f):
    B, H, S, dk = q.shape
    dv = v.shape[-1]
    C = min(HGRN_CHUNK, S)
    NC = S // C
    to_chunks = lambda a: jnp.moveaxis(a.reshape(B, H, NC, C, a.shape[-1]), 2, 0)
    causal = jnp.tril(jnp.ones((C, C), dtype=bool))[:, :, None]

    def step(state, xs):
        qc, kc, vc, gc = xs
        b = jnp.cumsum(gc, axis=2)
        diff = b[:, :, :, None, :] - b[:, :, None, :, :]
        decay = jnp.exp(jnp.where(causal, diff, -jnp.inf))
        attn = jnp.sum(qc[:, :, :, None, :] * decay * kc[:, :, None, :, :], axis=-1)
        o = (jnp.einsum('bhnm,bhme->bhne', attn, vc)
             + jnp.einsum('bhnd,bhde->bhne', qc * jnp.exp(b), state))
        b_last = b[:, :, -1:, :]
        new_state = (jnp.exp(b_last[:, :, 0, :])[..., None] * state
                     + jnp.einsum('bhmd,bhme->bhde', kc * jnp.exp(b_last - b), vc))
        return new_state, o

    _, o = lax.scan(step, jnp.zeros((B, H, dk, dv), jnp.float32),
                    (to_chunks(q), to_chunks(k), to_chunks(v), to_chunks(log_f)))
    return jnp.moveaxis(o, 0, 2).reshape(B, H, S, dv)

def hgrn2_mixer(h, w_in, w_out, norm_g, lb):
    B, S, _ = h.shape
    proj = (h @ w_in).astype(jnp.float32)
    qp, fp, ip, gp = _split(proj, ODD_SIZES)
    heads = lambda a: jnp.transpose(a.reshape(B, S, HGRN_HEADS, -1), (0, 2, 1, 3))
    lb = jnp.maximum(lb, 0.0)
    log_f = jnp.logaddexp(jnp.log(lb), jnp.log1p(-lb) + jax.nn.log_sigmoid(fp))
    k = (1.0 - lb) * jax.nn.sigmoid(-fp)
    q = jax.nn.silu(qp) * HGRN_DK ** -0.5
    o = hgrn2_chunkwise(heads(q), heads(k), heads(ip), heads(log_f))
    o = o * lax.rsqrt(jnp.mean(o * o, axis=-1, keepdims=True) + EPS) * norm_g.astype(jnp.float32)
    o = jnp.transpose(o, (0, 2, 1, 3)).reshape(B, S, ODD_MIX) * jax.nn.sigmoid(gp)
    return o.astype(h.dtype) @ w_out

def swiglu(h, w1, w3, w2):
    return (jax.nn.silu(h @ w1) * (h @ w3)) @ w2

def first_inputs(seed: int = 0) -> dict:
    key = jax.random.key(seed)
    ks = jax.random.split(key, 20)
    nrm = lambda k, shape, s: jax.random.normal(k, shape, jnp.float32) * s
    return {
        "x": nrm(ks[0], (BATCH, SEQ, D_MODEL), 1.0),
        "norm_mix_g": 1.0 + nrm(ks[1], (DEPTH, D_MODEL), 0.05),
        "norm_ffn_g": 1.0 + nrm(ks[2], (DEPTH, D_MODEL), 0.05),
        "final_norm_g": 1.0 + nrm(ks[3], (D_MODEL,), 0.05),
        "even_w_in": nrm(ks[4], (N_EVEN, D_MODEL, EVEN_IN), D_MODEL ** -0.5),
        "even_w_out": nrm(ks[5], (N_EVEN, EVEN_MIX, D_MODEL), EVEN_MIX ** -0.5),
        "cmp_pos_k": nrm(ks[6], (N_EVEN, CMP_BLOCK, NSA_HD), 0.1),
        "cmp_w1_k": nrm(ks[7], (N_EVEN, CMP_BLOCK * NSA_HD, NSA_HD), (CMP_BLOCK * NSA_HD) ** -0.5),
        "cmp_w2_k": nrm(ks[8], (N_EVEN, NSA_HD, NSA_HD), NSA_HD ** -0.5),
        "cmp_pos_v": nrm(ks[9], (N_EVEN, CMP_BLOCK, NSA_HD), 0.1),
        "cmp_w1_v": nrm(ks[10], (N_EVEN, CMP_BLOCK * NSA_HD, NSA_HD), (CMP_BLOCK * NSA_HD) ** -0.5),
        "cmp_w2_v": nrm(ks[11], (N_EVEN, NSA_HD, NSA_HD), NSA_HD ** -0.5),
        "odd_w_in": nrm(ks[12], (N_ODD, D_MODEL, ODD_IN), D_MODEL ** -0.5),
        "odd_w_out": nrm(ks[13], (N_ODD, ODD_MIX, D_MODEL), ODD_MIX ** -0.5),
        "hgrn_norm_g": 1.0 + nrm(ks[14], (N_ODD, HGRN_DV), 0.05),
        "hgrn_lb_logits": nrm(ks[15], (N_ODD, HGRN_HEADS * HGRN_DK), 1.0),
        "ffn_w1": nrm(ks[16], (DEPTH, D_MODEL, D_FF), D_MODEL ** -0.5),
        "ffn_w3": nrm(ks[17], (DEPTH, D_MODEL, D_FF), D_MODEL ** -0.5),
        "ffn_w2": nrm(ks[18], (DEPTH, D_FF, D_MODEL), D_FF ** -0.5),
    }

def first_block(x, norm_mix_g, norm_ffn_g, final_norm_g, even_w_in, even_w_out,
              cmp_pos_k, cmp_w1_k, cmp_w2_k, cmp_pos_v, cmp_w1_v, cmp_w2_v,
              odd_w_in, odd_w_out, hgrn_norm_g, hgrn_lb_logits,
              ffn_w1, ffn_w3, ffn_w2):
    lb_sm = jax.nn.softmax(hgrn_lb_logits.astype(jnp.float32), axis=0)
    lb_all = jnp.cumsum(lb_sm, axis=0) - lb_sm[0:1]
    for layer in range(DEPTH):
        h = rmsnorm(x, norm_mix_g[layer])
        j = layer // 2
        if layer % 2 == 0:
            mix = retention_nsa_mixer(h, even_w_in[j], even_w_out[j],
                                      cmp_pos_k[j], cmp_w1_k[j], cmp_w2_k[j],
                                      cmp_pos_v[j], cmp_w1_v[j], cmp_w2_v[j])
        else:
            mix = hgrn2_mixer(h, odd_w_in[j], odd_w_out[j], hgrn_norm_g[j], lb_all[j])
        x = x + mix.astype(x.dtype)
        h = rmsnorm(x, norm_ffn_g[layer])
        x = x + swiglu(h, ffn_w1[layer], ffn_w3[layer], ffn_w2[layer]).astype(x.dtype)
    return rmsnorm(x, final_norm_g)


CHUNK = 64
N_A_LAYERS = DEPTH // 2
N_B_LAYERS = DEPTH - N_A_LAYERS
A_HEADS = 8
A_HEAD_DIM = D_MODEL // (2 * A_HEADS)
B_HEADS = 16
B_HEAD_DIM = D_MODEL // B_HEADS
LEFT_CHUNKS = 8
BAND_CHUNKS = LEFT_CHUNKS + 1
MAX_REL_DIST = 256
D_FF_2 = -(-8 * D_MODEL // (3 * 256)) * 256
ROPE_THETA = 10000.0
LN_EPS = 1e-5
SUBLN_EPS = 1e-5
DEEPNORM_ALPHA = (2 * DEPTH) ** 0.25
DEEPNORM_BETA = (8 * DEPTH) ** -0.25


def layer_norm(x, g, b):
    xf = x.astype(jnp.float32)
    mu = jnp.mean(xf, axis=-1, keepdims=True)
    var = jnp.mean(jnp.square(xf - mu), axis=-1, keepdims=True)
    y = (xf - mu) * lax.rsqrt(var + LN_EPS) * g.astype(jnp.float32) + b.astype(jnp.float32)
    return y.astype(x.dtype)

def rms_norm(x, g):
    xf = x.astype(jnp.float32)
    y = xf * lax.rsqrt(jnp.mean(jnp.square(xf), axis=-1, keepdims=True) + SUBLN_EPS)
    return (y * g.astype(jnp.float32)).astype(x.dtype)

def rope_tables(seq, dim):
    inv = ROPE_THETA ** (-jnp.arange(0, dim, 2, dtype=jnp.float32) / dim)
    ang = jnp.arange(seq, dtype=jnp.float32)[:, None] * inv[None, :]
    return jnp.cos(ang), jnp.sin(ang)

def apply_rope(x, cos, sin):
    half = x.shape[-1] // 2
    x1, x2 = x[..., :half], x[..., half:]
    cos = cos.astype(x.dtype)
    sin = sin.astype(x.dtype)
    return jnp.concatenate([x1 * cos - x2 * sin, x1 * sin + x2 * cos], axis=-1)

def lambda_init_fn(layer_idx):
    return 0.8 - 0.6 * math.exp(-0.3 * layer_idx)

def diff_attention(x, w_qkv, lam_params, subln_g, w_o, lambda_init):
    b, s, _ = x.shape
    qkv = x @ w_qkv
    q, k, v = jnp.split(qkv, 3, axis=-1)
    q = q.reshape(b, s, A_HEADS, 2, A_HEAD_DIM)
    k = k.reshape(b, s, A_HEADS, 2, A_HEAD_DIM)
    v = v.reshape(b, s, A_HEADS, 2 * A_HEAD_DIM)
    cos, sin = rope_tables(s, A_HEAD_DIM)
    cos = cos[:, None, None, :]
    sin = sin[:, None, None, :]
    q = apply_rope(q, cos, sin) * (A_HEAD_DIM ** -0.5)
    k = apply_rope(k, cos, sin)
    lp = lam_params.astype(jnp.float32)
    lam = jnp.exp(jnp.sum(lp[0] * lp[1])) - jnp.exp(jnp.sum(lp[2] * lp[3])) + lambda_init
    chunk_id = jnp.arange(s) // CHUNK
    neg = jnp.finfo(jnp.float32).min
    outs = []
    for i in range(s // Q_BLOCK):
        q0 = i * Q_BLOCK
        kend = q0 + Q_BLOCK
        sc = jnp.einsum('bqhmd,bkhmd->bhmqk', q[:, q0:kend], k[:, :kend],
                        preferred_element_type=jnp.float32)
        allowed = chunk_id[None, :kend] <= chunk_id[q0:kend, None]
        p = jax.nn.softmax(jnp.where(allowed, sc, neg), axis=-1)
        a = p[:, :, 0] - lam * p[:, :, 1]
        outs.append(jnp.einsum('bhqk,bkhe->bqhe', a.astype(v.dtype), v[:, :kend]))
    o = jnp.concatenate(outs, axis=1)
    o = rms_norm(o, subln_g) * (1.0 - lambda_init)
    return o.reshape(b, s, D_MODEL) @ w_o

def shared_kv_band(x, kv_w):
    b, s, _ = x.shape
    nc = s // CHUNK
    kv = x @ kv_w
    k, v = jnp.split(kv, 2, axis=-1)
    k = k.reshape(b, nc, CHUNK, B_HEADS, B_HEAD_DIM)
    v = v.reshape(b, nc, CHUNK, B_HEADS, B_HEAD_DIM)
    pad = ((0, 0), (LEFT_CHUNKS, 0), (0, 0), (0, 0), (0, 0))
    kp = jnp.pad(k, pad)
    vp = jnp.pad(v, pad)
    k_band = jnp.concatenate([kp[:, j:j + nc] for j in range(BAND_CHUNKS)], axis=2)
    v_band = jnp.concatenate([vp[:, j:j + nc] for j in range(BAND_CHUNKS)], axis=2)
    band_chunk = jnp.arange(BAND_CHUNKS * CHUNK) // CHUNK
    band_valid = (jnp.arange(nc)[:, None] - LEFT_CHUNKS + band_chunk[None, :]) >= 0
    return k_band, v_band, band_valid

def chunk_attention(x, k_band, v_band, band_valid, w_q, rel_table, w_o):
    b, s, _ = x.shape
    nc = s // CHUNK
    q = (x @ w_q).reshape(b, nc, CHUNK, B_HEADS, B_HEAD_DIM) * (B_HEAD_DIM ** -0.5)
    rel = (jnp.arange(BAND_CHUNKS * CHUNK)[None, :] - LEFT_CHUNKS * CHUNK
           - jnp.arange(CHUNK)[:, None])
    idx = jnp.clip(rel, -MAX_REL_DIST, MAX_REL_DIST) + MAX_REL_DIST
    bias = rel_table[:, idx].astype(jnp.float32)
    sc = jnp.einsum('bnqhd,bnkhd->bhnqk', q, k_band,
                    preferred_element_type=jnp.float32) + bias[:, None]
    sc = jnp.where(band_valid[:, None, :], sc, jnp.finfo(jnp.float32).min)
    p = jax.nn.softmax(sc, axis=-1)
    o = jnp.einsum('bhnqk,bnkhd->bnqhd', p.astype(v_band.dtype), v_band)
    return o.reshape(b, s, D_MODEL) @ w_o

def swiglu_2(x, w_in, w_out):
    gate, up = jnp.split(x @ w_in, 2, axis=-1)
    return (jax.nn.silu(gate) * up) @ w_out

def second_inputs(seed: int = 0) -> dict:
    key = jax.random.key(seed)
    ks = jax.random.split(key, 14)
    f32 = jnp.float32
    d = D_MODEL
    nrm = lambda k, shape, sc: jax.random.normal(k, shape, f32) * sc
    return {
        "x": nrm(ks[0], (BATCH, SEQ, d), 1.0),
        "a_w_qkv": nrm(ks[1], (N_A_LAYERS, d, 3 * d), d ** -0.5),
        "a_lambda": nrm(ks[2], (N_A_LAYERS, 4, A_HEAD_DIM), 0.1),
        "a_subln_g": 1.0 + nrm(ks[3], (N_A_LAYERS, 2 * A_HEAD_DIM), 0.02),
        "a_w_o": nrm(ks[4], (N_A_LAYERS, d, d), d ** -0.5 * DEEPNORM_BETA),
        "kv_w": nrm(ks[5], (d, 2 * d), d ** -0.5),
        "b_w_q": nrm(ks[6], (N_B_LAYERS, d, d), d ** -0.5),
        "b_rel_bias": nrm(ks[7], (N_B_LAYERS, B_HEADS, 2 * MAX_REL_DIST + 1), 0.2),
        "b_w_o": nrm(ks[8], (N_B_LAYERS, d, d), d ** -0.5 * DEEPNORM_BETA),
        "ln_g": 1.0 + nrm(ks[9], (DEPTH, 2, d), 0.02),
        "ln_b": nrm(ks[10], (DEPTH, 2, d), 0.02),
        "ffn_w_in": nrm(ks[11], (DEPTH, d, 2 * D_FF_2), d ** -0.5),
        "ffn_w_out": nrm(ks[12], (DEPTH, D_FF_2, d), D_FF_2 ** -0.5 * DEEPNORM_BETA),
    }

def second_block(x, a_w_qkv, a_lambda, a_subln_g, a_w_o, kv_w, b_w_q, b_rel_bias, b_w_o,
              ln_g, ln_b, ffn_w_in, ffn_w_out):
    k_band = v_band = band_valid = None
    for l in range(DEPTH):
        if l < N_A_LAYERS:
            mix = diff_attention(x, a_w_qkv[l], a_lambda[l], a_subln_g[l], a_w_o[l],
                                 lambda_init_fn(l))
        else:
            if l == N_A_LAYERS:
                k_band, v_band, band_valid = shared_kv_band(x, kv_w)
            j = l - N_A_LAYERS
            mix = chunk_attention(x, k_band, v_band, band_valid, b_w_q[j], b_rel_bias[j], b_w_o[j])
        x = layer_norm(DEEPNORM_ALPHA * x + mix, ln_g[l, 0], ln_b[l, 0])
        x = layer_norm(DEEPNORM_ALPHA * x + swiglu_2(x, ffn_w_in[l], ffn_w_out[l]), ln_g[l, 1], ln_b[l, 1])
    return x


def setup_inputs(seed=0):
    out = dict(first_inputs(seed))
    for name, value in second_inputs(seed + 1).items():
        if name != "x":
            out[name + "_2"] = value
    return out


def reference(
    x, norm_mix_g, norm_ffn_g, final_norm_g, even_w_in, even_w_out, cmp_pos_k, cmp_w1_k,
    cmp_w2_k, cmp_pos_v, cmp_w1_v, cmp_w2_v, odd_w_in, odd_w_out, hgrn_norm_g, hgrn_lb_logits,
    ffn_w1, ffn_w3, ffn_w2, a_w_qkv_2, a_lambda_2, a_subln_g_2, a_w_o_2, kv_w_2, b_w_q_2,
    b_rel_bias_2, b_w_o_2, ln_g_2, ln_b_2, ffn_w_in_2, ffn_w_out_2,
):
    x = first_block(
        x, norm_mix_g, norm_ffn_g, final_norm_g, even_w_in, even_w_out, cmp_pos_k, cmp_w1_k,
        cmp_w2_k, cmp_pos_v, cmp_w1_v, cmp_w2_v, odd_w_in, odd_w_out, hgrn_norm_g,
        hgrn_lb_logits, ffn_w1, ffn_w3, ffn_w2,
    )
    return second_block(
        x, a_w_qkv_2, a_lambda_2, a_subln_g_2, a_w_o_2, kv_w_2, b_w_q_2, b_rel_bias_2, b_w_o_2,
        ln_g_2, ln_b_2, ffn_w_in_2, ffn_w_out_2,
    )


_drawn_inputs = setup_inputs


def setup_inputs(seed=0):
    import zlib

    import numpy as np

    out = dict(_drawn_inputs(seed))
    spreads = {}
    factors = {'cmp_pos_k': 8.0, 'a_subln_g_2': 8.0, 'b_rel_bias_2': 5.777}
    for name, (base, spread) in spreads.items():
        noise = np.random.default_rng([zlib.crc32(name.encode()), seed]).standard_normal(out[name].shape)
        drawn = base * np.exp(spread * noise) if base else spread * noise
        out[name] = __import__('jax').numpy.asarray(drawn.astype(out[name].dtype))
    for name, factor in factors.items():
        out[name] = (out[name] * factor).astype(out[name].dtype)
    return out
```

```python
from collections import deque
from contextlib import ExitStack

import numpy as np

import concourse.bass as bass
from concourse import mybir

ALU = mybir.AluOpType
ACT = mybir.ActivationFunctionType
X_AX = mybir.AxisListType.X
F = mybir.dt.float32
R = mybir.dt.float32r

D = 1024
FF = 2816
NEG = -1.0e30
ALPHA = 4 ** 0.25
LAM0 = 0.8 - 0.6
EPS = 1e-6
LN_EPS = 1e-5

LEVELS = [64, 32, 16, 8, 4, 2, 1]
NLEV = len(LEVELS)

GM0, GF0, GM1, GF1, POSK, POSV = 0, 8, 16, 24, 32, 48
NCOLP = 64
C_ID, C_CM, C_KM, C_CMP, C_RC, C_RS, C_AC, C_AS = 0, 128, 384, 640, 672, 928, 1184, 1312
NCONST = 1440
NSMALL = 960


def ranges(*parts):
    return np.concatenate([np.arange(a, a + n) for a, n in parts])


def blocks_of(width):
    return [min(512, width - c) for c in range(0, width, 512)]


E_COLS = ranges((2048, 512), (2560, 512), (3072, 280), (0, 512), (512, 512), (1024, 512), (1536, 512))
E_BLOCKS = [512, 512, 280, 512, 512, 512, 512]
H_COLS = ranges(*[(a + 256 * u, 256) for u in range(4) for a in (0, 1024, 2048, 3072)])
A_COLS = ranges(*[p for v in range(2) for p in (
    (512 * v, 256), (1024 + 512 * v, 256), (2048 + 512 * v, 512), (512 * v + 256, 256), (1280 + 512 * v, 256))])
WEIGHTS = {
    "w_e": (D, E_BLOCKS), "w_eo": (D, [512] * 2), "w_h": (D, [512] * 8), "w_ho": (D, [512] * 2),
    "w_a": (D, [512] * 6), "w_ao": (D, [512] * 2), "w_b": (D, [512] * 6), "w_bo": (D, [512] * 2),
    "u0": (D, blocks_of(FF)), "u1": (D, blocks_of(FF)), "u2": (D, blocks_of(FF)), "u3": (D, blocks_of(FF)),
    "g0": (D, blocks_of(FF)), "g1": (D, blocks_of(FF)), "g2": (D, blocks_of(FF)), "g3": (D, blocks_of(FF)),
    "d0": (FF, [512] * 2), "d1": (FF, [512] * 2), "d2": (FF, [512] * 2), "d3": (FF, [512] * 2),
}


def chunks_of(K, width):
    n = K // 128
    per = 1024 // width
    return [(k, min(per, n - k)) for k in range(0, n, per)]


def lay_out(w, name):
    K, blocks = WEIGHTS[name]
    parts, c = [], 0
    for width in blocks:
        for k, n in chunks_of(K, width):
            tile = w[128 * k:128 * (k + n), c:c + width].reshape(n, 128, width)
            parts.append(np.ascontiguousarray(tile.transpose(1, 0, 2)).reshape(-1))
        c += width
    return np.concatenate(parts)


def shape_constants():
    p = np.arange(128)[:, None]
    c = np.zeros((128, NCONST), np.float32)
    c[:, C_ID:C_ID + 128] = np.eye(128)
    j = np.arange(128)[None, :]
    c[:, C_CM + 128:C_CM + 256] = np.where(j <= p, 0.0, NEG)
    c[:, C_KM + 128:C_KM + 256] = np.where(j // 64 <= p // 64, 0.0, NEG)
    for t in range(2):
        n = np.arange(16)[None, :]
        c[:, C_CMP + 16 * t:C_CMP + 16 * t + 16] = np.where(16 * n + 31 <= 128 * t + p, 0.0, NEG)
    for half, at_c, at_s in ((64, C_RC, C_RS), (32, C_AC, C_AS)):
        inv = (np.float32(10000.0) ** (-np.arange(half, dtype=np.float32) / np.float32(half))).astype(np.float32)
        for t in range(2):
            ang = ((128 * t + np.arange(128, dtype=np.float32))[:, None] * inv[None, :]).astype(np.float32)
            co, si = np.cos(ang.astype(np.float64)), np.sin(ang.astype(np.float64))
            w = 2 * half
            c[:, at_c + w * t:at_c + w * t + w] = np.concatenate([co, co], 1)
            c[:, at_s + w * t:at_s + w * t + w] = np.concatenate([-si, si], 1)
    ret = np.zeros((128, 4, 256), np.float32)
    t = np.arange(256)[None, :]
    for h in range(4):
        lg = np.log(1.0 - 2.0 ** (-5.0 - h))
        ret[:, h] = np.where(t >= p, np.exp(lg * np.maximum(t - p, 0)), 0.0) * 128 ** -0.5
    s = np.arange(128)[:, None]
    n = np.arange(128)[None, :]
    hw = np.zeros((128, 9, 128), np.float32)
    hm = np.zeros((128, 8, 128), np.float32)
    for i, L in enumerate(LEVELS):
        mid = n // (2 * L) * 2 * L + L - 1
        right = n % (2 * L) >= L
        hw[:, i] = np.where(right, (s > mid) & (s <= n), (s > n) & (s <= mid))
        m = s
        hm[:, i] = (m // (2 * L) == n // (2 * L)) & (m % (2 * L) < L) & (n % (2 * L) >= L)
    hw[:, 7] = s > n
    hw[:, 8] = s <= n
    hm[:, 7] = s == n
    return c, ret.reshape(128, 1024), np.concatenate([hw.reshape(128, -1), hm.reshape(128, -1)], 1)


class Calls:

    def matmul(self, *a, **k):
        return lambda e: e.matmul(*a, **k)

    def transpose(self, *a, **k):
        return lambda e: e.transpose(*a, **k)

    def activation(self, *a, **k):
        return lambda e: e.activation(*a, **k)

    def tensor_tensor(self, *a, **k):
        return lambda e: e.tensor_tensor(*a, **k)

    def tensor_scalar(self, *a, **k):
        return lambda e: e.tensor_scalar(*a, **k)

    def scalar_tensor_tensor(self, *a, **k):
        return lambda e: e.scalar_tensor_tensor(*a, **k)

    def tensor_reduce(self, *a, **k):
        return lambda e: e.tensor_reduce(*a, **k)

    def tensor_copy(self, *a, **k):
        return lambda e: e.tensor_copy(*a, **k)

    def reciprocal(self, *a, **k):
        return lambda e: e.reciprocal(*a, **k)

    def bn_stats(self, *a, **k):
        return lambda e: e.bn_stats(*a, **k)

    def bn_aggr(self, *a, **k):
        return lambda e: e.bn_aggr(*a, **k)

    def memset(self, *a, **k):
        return lambda e: e.memset(*a, **k)

    def dma_start(self, *a, **k):
        return lambda e: e.dma_start(*a, **k)


CALLS = Calls()


class Op:

    def __init__(self, fn, waits):
        self.fn, self.waits, self.sem, self.value, self.signals = fn, waits, None, 0, False


class Queues:

    def __init__(self):
        self.q = {k: [] for k in ("sync", "tensor", "vector", "scalar", "gpsimd")}

    def add(self, eng, make, *waits):
        fn = make(CALLS)
        flat = []
        for w in waits:
            flat += list(w) if isinstance(w, (list, tuple)) else [w] if w is not None else []
        for w in flat:
            w.signals = True
        op = Op(fn, flat)
        self.q[eng].append(op)
        return op

    def pe(self, fn, *w):
        return self.add("tensor", fn, *w)

    def act(self, fn, *w):
        return self.add("scalar", fn, *w)

    def dve(self, fn, *w):
        return self.add("vector", fn, *w)

    def pool(self, fn, *w):
        return self.add("gpsimd", fn, *w)

    def dma(self, eng, sem, out, src, *w):
        op = self.add(eng, lambda e: e.dma_start(out, src), *w)
        sem[1] += 16
        op.sem, op.value = sem[0], sem[1]
        return op

    def count(self, sems):
        for k, ops in self.q.items():
            n = 0
            for op in ops:
                if op.sem is None and op.signals:
                    n += 1
                    op.sem, op.value = sems[k], n

    def emit(self, k, e):
        seen = {}
        for op in self.q[k]:
            for w in op.waits:
                key = w.sem.name
                if seen.get(key, 0) < w.value:
                    e.wait_ge(w.sem, w.value)
                    seen[key] = w.value
            ins = op.fn(e)
            if op.sem is not None:
                ins.then_inc(op.sem, 16 if op.value and k in ("sync", "gpsimd") and op.sem.name.startswith("d_") else 1)


class Pair:

    def __init__(self, tile):
        self.t, self.free = tile, []


def program(nc, a, out):
    ctx = ExitStack()
    with ctx:
        def sb(name, shape, dt=F, stack=ctx):
            return stack.enter_context(nc.sbuf_tensor(name, shape, dt))

        def sem(name):
            return ctx.enter_context(nc.semaphore(name))

        Q = Queues()
        NR, NH, LA = 5, 4, 2

        G = [Pair(ctx.enter_context(nc.psum_tensor(f"G{i}", [128, 1024], F))) for i in range(2)]
        A = [Pair(ctx.enter_context(nc.psum_tensor(f"A{i}", [128, 1024], F))) for i in range(2)]

        raw = [sb(f"raw{i}", [128, 1024]) for i in range(NR)]
        whi = [sb(f"whi{i}", [128, 1024], R) for i in range(NH)]
        wlo = [sb(f"wlo{i}", [128, 1024], R) for i in range(NH)]
        X = sb("X", [128, 2, D])
        xh = sb("xh", [128, 8, 256], R)
        xl = sb("xl", [128, 8, 256], R)
        CN = sb("CN", [128, NCONST])
        CP = sb("CP", [128, NCOLP])
        GB = sb("GB", [128, 2, D])
        LC = sb("LC", [128, 2176])
        SM = sb("SM", [128, NSMALL])
        MSQ = [sb(f"MSQ{t}", [128, 512]) for t in range(2)]
        W = [[sb(f"W{s}{i}", [128, 1024]) for i in range(3)] for s in range(2)]

        shared = ExitStack()
        mh = sb("mh", [128, 8, 256], R, shared)
        ml = sb("ml", [128, 8, 256], R, shared)
        MX = sb("MX", [128, 2, D], F, shared)
        PJ = sb("PJ", [128, 2, 3352], F, shared)
        mixer = ExitStack()
        shared.enter_context(mixer)
        e0 = ExitStack()
        QT = sb("QT", [128, 4, 256], F, e0)
        KT = sb("KT", [128, 4, 256], F, e0)
        Z = sb("Z", [128, 4, 256], F, e0)
        w1c = sb("w1c", [128, 2, 16 * 64], F, e0)
        w2c = sb("w2c", [64, 256], F, e0)
        CK = sb("CK", [128, 512], F, e0)
        e0.close()
        e1 = ExitStack()
        lfh = sb("lfh", [128, 2, 512], R, e1)
        lfl = sb("lfl", [128, 2, 512], R, e1)
        Wr = sb("Wr", [128, 9 * 128], R, e1)
        HN = sb("HN", [128, D + 128], F, e1)
        HQ = [sb(f"HQ{s}", [128, 768], F, e1) for s in range(2)]
        e1.close()
        e2 = ExitStack()
        QTa = sb("QTa", [128, 8, 256], F, e2)
        KTa = sb("KTa", [128, 8, 256], F, e2)
        AG = sb("AG", [128, 384], F, e2)
        TB = [sb(f"TB{s}", [128, 1024], F, e2) for s in range(2)]
        e2.close()
        shared.close()
        ffn = ExitStack()
        hh = sb("hh", [128, 22, 256], R, ffn)
        hl = sb("hl", [128, 22, 256], R, ffn)
        sa = [sb(f"sa{i}", [128, 2, 512], F, ffn) for i in range(2)]
        ffn.close()

        sems = {k: sem(f"s_{k}") for k in Q.q}
        s_raw = [[sem(f"d_raw{i}"), 0] for i in range(NR)]
        s_cn = [sem("d_cn"), 0]
        s_lc = [sem("d_lc"), 0]
        s_e = [sem("d_e"), 0]
        s_gb = [sem("d_gb"), 0]
        s_h = [sem("d_h"), 0]
        s_a = [sem("d_a"), 0]
        s_out = [sem("d_out"), 0]

        used = [0]

        def small(n):
            at = used[0]
            used[0] += n
            assert used[0] <= NSMALL, used
            return SM[:, at:at + n]

        ld_x = Q.dma("sync", [sem("d_x"), 0], X[:, :, :], a["x"].rearrange("(t p) d -> p t d", p=128))
        Q.dma("sync", s_cn, CN[:, :], a["consts"])
        ld_cn = Q.dma("sync", s_cn, CP[:, :], a["cols"])
        ld_ret = Q.dma("gpsimd", s_lc, LC[:, 0:1024], a["ret"])
        Q.dma("gpsimd", s_e, w1c[:, 0, :], a["cw1k"])
        Q.dma("gpsimd", s_e, w1c[:, 1, :], a["cw1v"])
        Q.dma("gpsimd", s_e, w2c[:, 0:64], a["cw2k"])
        Q.dma("gpsimd", s_e, w2c[:, 64:128], a["cw2k"])
        ld_e = Q.dma("gpsimd", s_e, w2c[:, 128:192], a["cw2v"])
        ident = CN[:, C_ID:C_ID + 128]

        consts = small(4)
        c_eps = [Q.dve(lambda e: e.memset(consts[:, 0:1], EPS)),
                 Q.dve(lambda e: e.memset(consts[:, 1:2], LN_EPS))]

        stream = []
        order = ["w_e", "w_eo", ("g0", "u0"), "d0", "w_h", "w_ho", ("g1", "u1"), "d1",
                 "w_a", "w_ao", ("g2", "u2"), "d2", "w_b", "w_bo", ("g3", "u3"), "d3"]
        for o in order:
            names = o if isinstance(o, tuple) else (o,)
            at = dict.fromkeys(names, 0)
            K, blocks = WEIGHTS[names[0]]
            for width in blocks:
                for name in names:
                    for k, n in chunks_of(K, width):
                        stream.append((name, at[name], k, n, width))
                        at[name] += 128 * n * width
        hi_op, lo_op, pe_op = [], [], []

        def ensure(upto):
            while len(hi_op) <= min(upto, len(stream) - 1):
                c = len(hi_op)
                name, at, _, n, width = stream[c]
                r, h, m = raw[c % NR], c % NH, n * width
                src = a[name][at:at + 128 * m].rearrange("(p m) -> p m", p=128)
                ld = Q.dma("sync", s_raw[c % NR], r[:, 0:m], src, lo_op[c - NR] if c >= NR else None)
                gone = pe_op[c - NH] if c >= NH else None
                hi_op.append(Q.act(lambda e, h=h, r=r, m=m: e.activation(whi[h][:, 0:m], r[:, 0:m], ACT.Copy),
                                   ld, gone))
                lo_op.append(Q.dve(lambda e, h=h, r=r, m=m: e.tensor_tensor(
                    wlo[h][:, 0:m], r[:, 0:m], whi[h][:, 0:m].bitcast(F), ALU.subtract), hi_op[c]))

        jobs = deque()
        running = [None, None]

        def tick():
            moved = False
            for s in range(2):
                if running[s] is None and jobs:
                    running[s] = jobs.popleft()(A[s], W[s], s)
                if running[s] is not None:
                    moved = True
                    try:
                        next(running[s])
                    except StopIteration:
                        running[s] = None
            return moved

        def drain():
            while tick():
                pass

        def until(store, key, n=1):
            guard = 0
            while len(store.get(key, ())) < n:
                guard += 1
                assert guard < 2000 and (tick() or guard < 2000), key
            return store[key]

        def have(store, key, n=1):
            guard = 0
            while len(store.get(key, ())) < n:
                guard += 1
                assert guard < 5000, key
                yield
            return store[key]

        turn = [0]
        cur = [0]

        def product_block(sh, sl, ready, nready):
            pair = G[turn[0] % 2]
            turn[0] += 1
            assert pair.free is not None
            free, pair.free = pair.free, None
            K, _ = WEIGHTS[stream[cur[0]][0]]
            name, _, _, _, width = stream[cur[0]]
            for k0, n in chunks_of(K, width):
                c = cur[0]
                cur[0] += 1
                ensure(c + LA)
                h = c % NH
                for j in range(n):
                    kt = k0 + j
                    ok = until(ready, kt, nready)
                    for t in range(2):
                        o = pair.t[:, 512 * t:512 * t + width]
                        xs = slice(128 * t, 128 * t + 128)
                        ws = slice(j * width, (j + 1) * width)
                        first, last = kt == 0, kt == K // 128 - 1
                        for n3, (l, r) in enumerate(((sh, whi), (sh, wlo), (sl, whi))):
                            w = (hi_op[c], ok, free) if n3 != 1 else (lo_op[c],)
                            op = Q.pe(lambda e, o=o, l=l, r=r, kt=kt, xs=xs, ws=ws, h=h, s=first and n3 == 0, z=last and n3 == 2:
                                      e.matmul(o, l[:, kt, xs], r[h][:, ws], start=s, stop=z), *w)
                pe_op.append(op)
                tick()
            return pair, op

        def turn_over(src, t, k0, n, dh, dl, ready, waits, gcol=None):
            def job(pair, w, s):
                for i in range(n):
                    op = Q.pe(lambda e, i=i: e.transpose(pair.t[:, 128 * i:128 * i + 128],
                                                         src[:, 128 * i:128 * i + 128], ident),
                              waits, pair.free, ld_cn)
                yield
                ps = pair.t[:, 0:128 * n].rearrange("p (k c) -> p k c", k=n)
                oh = dh[:, k0:k0 + n, 128 * t:128 * t + 128]
                ol = dl[:, k0:k0 + n, 128 * t:128 * t + 128]
                if gcol is not None:
                    tmp = w[0][:, 0:128 * n].rearrange("p (k c) -> p k c", k=n)
                    g = CP[:, gcol + k0:gcol + k0 + n].unsqueeze(2).to_broadcast([128, n, 128])
                    m = Q.dve(lambda e: e.tensor_tensor(tmp, ps, g, ALU.mult), op)
                    hi = Q.act(lambda e: e.activation(oh, tmp, ACT.Copy), m)
                    lo = Q.dve(lambda e: e.tensor_tensor(ol, tmp, oh.bitcast(F), ALU.subtract), hi)
                else:
                    hi = Q.act(lambda e: e.activation(oh, ps, ACT.Copy), op)
                    lo = Q.dve(lambda e: e.tensor_tensor(ol, ps, oh.bitcast(F), ALU.subtract), hi)
                pair.free = [lo]
                for k in range(k0, k0 + n):
                    ready.setdefault(k, []).extend([hi, lo])
                yield
            return job

        def rstd_of(ms, eps, scale, *waits):
            n = ms.shape[1]
            y = small(n)
            ln = Q.act(lambda e: e.activation(y, ms, ACT.Ln, scale=scale, bias=consts[:, eps:eps + 1]), c_eps, *waits)
            return y, Q.act(lambda e: e.activation(y, y, ACT.Exp, scale=-0.5), ln)

        junk = GB[:, 1, 0:512]

        class Rms:

            def __init__(self):
                self.ms = [small(2) for _ in range(2)]
                self.ops = [[], []]
                self.r = [None, None]

            def add(self, b, t, dst, *waits):
                op = Q.act(lambda e: e.activation(dst, X[:, t, 512 * b:512 * b + 512], ACT.Square,
                                                  accum_out=self.ms[t][:, b:b + 1]), *waits)
                self.ops[t].append(op)
                if len(self.ops[t]) == 2:
                    s = small(1)
                    m = Q.dve(lambda e: e.tensor_tensor(s, self.ms[t][:, 0:1], self.ms[t][:, 1:2], ALU.add), self.ops[t])
                    self.r[t] = rstd_of(s, 0, 1.0 / D, m)
                return op

        def residual(pair, op, b, alpha, waits=()):
            ops = []
            for t in range(2):
                x = X[:, t, 512 * b:512 * b + 512]
                ops.append(Q.dve(lambda e, t=t, x=x: e.scalar_tensor_tensor(
                    out=x, in0=x, scalar=alpha, in1=pair.t[:, 512 * t:512 * t + 512], op0=ALU.mult, op1=ALU.add),
                    op, waits))
            pair.free = list(ops)
            return ops

        def out_rms(src_h, src_l, ready, nready, gcol):
            nxt, rms = {}, Rms()
            for b in range(2):
                pair, op = product_block(src_h, src_l, ready, nready)
                xs = residual(pair, op, b, 1.0)
                for t in range(2):
                    if gcol is not None:
                        jobs.append(turn_over(X[:, t, 512 * b:512 * b + 512], t, 4 * b, 4, xh, xl, nxt, [xs[t]], gcol))
                    rms.add(b, t, MSQ[t][:, 0:512], xs[t], rms.ops[t])
            return nxt, rms

        gb_use = [[]]

        def load_gb(g, b=None):
            w = gb_use[0]
            op = Q.dma("gpsimd", s_gb, GB[:, 0, :], g.partition_broadcast(128), w)
            if b is not None:
                op = Q.dma("gpsimd", s_gb, GB[:, 1, :], b.partition_broadcast(128), w)
            return op

        def out_ln(src_h, src_l, ready, nready, gb, last=False):
            st = [small(12) for _ in range(2)]
            sts = [[], []]
            for b in range(2):
                pair, op = product_block(src_h, src_l, ready, nready)
                xs = residual(pair, op, b, ALPHA)
                for t in range(2):
                    sts[t].append(Q.dve(lambda e, t=t, b=b: e.bn_stats(st[t][:, 6 * b:6 * b + 6],
                                                                       X[:, t, 512 * b:512 * b + 512]), xs[t]))
            nxt, fin = {}, []
            drain()
            for t in range(2):
                mv = small(2)
                ag = Q.dve(lambda e, t=t, mv=mv: e.bn_aggr(mv, st[t]), sts[t])
                r, ro = rstd_of(mv[:, 1:2], 1, 1.0, ag)
                x = X[:, t, :]
                o = Q.dve(lambda e, x=x, mv=mv: e.scalar_tensor_tensor(
                    out=x, in0=x, scalar=mv[:, 0:1], in1=GB[:, 0, :], op0=ALU.subtract, op1=ALU.mult), ag, gb)
                o = Q.dve(lambda e, x=x, r=r: e.scalar_tensor_tensor(
                    out=x, in0=x, scalar=r, in1=GB[:, 1, :], op0=ALU.mult, op1=ALU.add), o, ro)
                fin.append(o)
                if not last:
                    jobs.append(turn_over(x, t, 0, 8, xh, xl, nxt, [o]))
            gb_use[0] = fin
            return nxt, fin

        def feed_forward(ready, rms):
            done = {}

            def finish(b, width, a_ops, s_, pair, op):
                ops = []
                for t in range(2):
                    h = s_[:, t, 0:width]
                    ps = pair.t[:, 512 * t:512 * t + width]
                    if rms is not None:
                        ops.append(Q.dve(lambda e, h=h, ps=ps, t=t: e.scalar_tensor_tensor(
                            out=h, in0=ps, scalar=rms.r[t][0], in1=h, op0=ALU.mult, op1=ALU.mult), op, a_ops[t]))
                    else:
                        ops.append(Q.dve(lambda e, h=h, ps=ps: e.tensor_tensor(h, ps, h, ALU.mult), op, a_ops[t]))
                pair.free = list(ops)
                for t in range(2):
                    jobs.append(turn_over(s_[:, t, 0:width], t, 4 * b, width // 128, hh, hl, done, [ops[t]]))

            for b, width in enumerate(blocks_of(FF)):
                s_ = sa[b % 2]
                pair, op = product_block(xh, xl, ready, 4)
                if b >= 2:
                    until(done, 4 * (b - 2), 4)
                a_ops = []
                for t in range(2):
                    o, ps = s_[:, t, 0:width], pair.t[:, 512 * t:512 * t + width]
                    sc = rms.r[t][0] if rms is not None else 1.0
                    a_ops.append(Q.act(lambda e, o=o, ps=ps, sc=sc: e.activation(o, ps, ACT.Silu, scale=sc), op,
                                       [rms.r[t][1]] if rms is not None else None,
                                       done[4 * (b - 2)] if b >= 2 else None))
                pair.free = list(a_ops)
                pair, op = product_block(xh, xl, ready, 4)
                finish(b, width, a_ops, s_, pair, op)
            return done

        def softmax4(pair, w, t, qs, ks, mask, scale, nk, stride, waits, mwaits=()):
            for i in range(4):
                at = 512 * (i % 2) + 256 * (i // 2)
                op = Q.pe(lambda e: e.matmul(pair.t[:, at:at + nk], qs[i], ks[i], start=True, stop=True),
                          waits, pair.free)
            yield
            S = w[0][:, 0:4 * stride].rearrange("p (h k) -> p h k", h=4)[:, :, 0:nk]
            mx, sm, rs = small(4), small(4), small(4)
            m = []
            for b in range(2):
                ps = pair.t[:, 512 * b:512 * b + 512].rearrange("p (h k) -> p h k", h=2)[:, :, 0:nk]
                m.append(Q.dve(lambda e: e.scalar_tensor_tensor(
                    out=S[:, b:4:2, :], in0=ps, scalar=scale, in1=mask[:, b:4:2, :],
                    op0=ALU.mult, op1=ALU.add), op, mwaits))
            r = Q.dve(lambda e: e.tensor_reduce(mx, S, X_AX, ALU.max), m)
            ng = Q.dve(lambda e: e.tensor_scalar(mx, mx, -1.0e20, -1.0, ALU.max, ALU.mult), r)
            ex = [Q.act(lambda e, i=i: e.activation(S[:, i, :], S[:, i, :], ACT.Exp, bias=mx[:, i:i + 1],
                                                    accum_out=sm[:, i:i + 1]), ng) for i in range(4)]
            g = Q.dve(lambda e: e.tensor_scalar(sm, sm, 1.0e-30, None, ALU.max), ex)
            rc = Q.dve(lambda e: e.reciprocal(rs, sm), g)
            yield
            return S, rs, ex, rc

        def weigh(pair, w, S, nk, vs, ow, waits, vwaits, n=4):
            nb = (nk + 127) // 128
            kp = min(nk, 128)
            for i in range(n):
                for b in range(nb):
                    at = (i * nb + b) * 128
                    op = Q.pe(lambda e, i=i, b=b, at=at: e.transpose(
                        pair.t[0:kp, at:at + 128], S[:, i, 128 * b:128 * b + kp], ident), waits)
            yield
            half = n * nb * 64
            e1_ = Q.act(lambda e: e.activation(w[1][0:kp, 0:half], pair.t[0:kp, 0:half], ACT.Copy), op)
            wt = e1_ if half < 512 else None
            e2_ = Q.dve(lambda e: e.tensor_copy(w[1][0:kp, half:2 * half], pair.t[0:kp, half:2 * half]), op, wt)
            yield
            for i in range(n):
                for b in range(nb):
                    at = (i * nb + b) * 128
                    op = Q.pe(lambda e, i=i, b=b, at=at: e.matmul(
                        pair.t[:, ow * i:ow * i + ow], w[1][0:kp, at:at + 128], vs[i][b],
                        start=b == 0, stop=b == nb - 1), e1_, e2_, vwaits)
            yield
            return op

        def sigmoid(dst, src, *waits):
            o = Q.dve(lambda e: e.tensor_scalar(dst, src, -1.0, 80.0, ALU.mult, ALU.min), *waits)
            o = Q.act(lambda e: e.activation(dst, dst, ACT.Exp), o)
            o = Q.act(lambda e: e.activation(dst, dst, ACT.Ln, bias=1.0), o)
            return Q.act(lambda e: e.activation(dst, dst, ACT.Exp, scale=-1.0), o)

        def evacuate(pair, op, at, width, rms, over=None):
            ops = []
            for t in range(2):
                o, ps = PJ[:, t, at:at + width], pair.t[:, 512 * t:512 * t + width]
                sc = rms.r[t][0] if rms is not None else 1.0
                ops.append(Q.act(lambda e, o=o, ps=ps, sc=sc: e.activation(o, ps, ACT.Copy, scale=sc), op,
                                 [rms.r[t][1]] if rms is not None else None, over))
            pair.free = list(ops)
            return ops

        def rotate(t, at, nh, half, tc, ts, *waits):
            w = 2 * half
            x = PJ[:, t, at:at + nh * w].rearrange("p (h c) -> p h c", h=nh)
            y = MX[:, t, 0:nh * w].rearrange("p (h c) -> p h c", h=nh)
            co = CN[:, tc + w * t:tc + w * t + w].unsqueeze(1).to_broadcast([128, nh, w])
            s0 = CN[:, ts + w * t:ts + w * t + half].unsqueeze(1).to_broadcast([128, nh, half])
            s1 = CN[:, ts + w * t + half:ts + w * t + w].unsqueeze(1).to_broadcast([128, nh, half])
            p = Q.dve(lambda e: e.tensor_tensor(y[:, :, 0:half], x[:, :, half:w], s0, ALU.mult), ld_cn, *waits)
            p = Q.dve(lambda e: e.tensor_tensor(y[:, :, half:w], x[:, :, 0:half], s1, ALU.mult), p)
            q = Q.dve(lambda e: e.tensor_tensor(x, x, co, ALU.mult), p)
            return Q.dve(lambda e: e.tensor_tensor(x, x, y, ALU.add), q)

        rms = Rms()
        nxt = {}
        for t in range(2):
            for b in range(2):
                rms.add(b, t, MSQ[t][:, :], ld_x, rms.ops[t])
                jobs.append(turn_over(X[:, t, 512 * b:512 * b + 512], t, 4 * b, 4, xh, xl, nxt, [ld_x], GM0))
        drain()

        got = {}
        NQ, N5, N6, RQ, RK, RV, RG = 0, 512, 1024, 1304, 1816, 2328, 2840

        def job_qt(t):
            def job(pair, w, s):
                for i in range(4):
                    op = Q.pe(lambda e, i=i: e.transpose(pair.t[:, 128 * i:128 * i + 128],
                                                         PJ[:, t, NQ + 128 * i:NQ + 128 * i + 128], ident),
                              got["nq"][t], pair.free)
                yield
                o = Q.act(lambda e: e.activation(QT[:, :, 128 * t:128 * t + 128],
                                                 pair.t[:, 0:512].rearrange("p (h c) -> p h c", h=4), ACT.Copy), op)
                pair.free = [o]
                got.setdefault("qt", []).append(o)
                yield
            return job

        def twice(ap):
            return ap.unsqueeze(1).to_broadcast([128, 2, 64])

        def job_twice(key, at, dst, i0, shifted):
            def job(pair, w, s):
                d = w[0][:, 0:512].rearrange("p (g t c) -> p g t c", g=2, t=2)
                cp = []
                first = Q.pe(lambda e: e.transpose(pair.t[:, 0:128], ident, ident), ld_cn, pair.free)
                for g in range(2):
                    for t in range(2):
                        dd = d[:, g, t, :].rearrange("p (u c) -> p u c", u=2)
                        cp.append(Q.dve(lambda e, g=g, t=t, dd=dd: e.tensor_copy(
                            dd, twice(PJ[:, t, at + 64 * g:at + 64 * g + 64])), first, got[key][t]))
                yield
                for g in range(2):
                    for t in range(2):
                        op = Q.pe(lambda e, g=g, t=t: e.transpose(
                            pair.t[:, 256 * g + 128 * t:256 * g + 128 * t + 128], d[:, g, t, :], ident), cp)
                yield
                ps = pair.t[:, 0:512].rearrange("p (g c) -> p g c", g=2)
                if shifted:
                    o1 = Q.act(lambda e: e.activation(dst[0:64, i0:i0 + 2, :], ps[0:64], ACT.Copy), op)
                    o2 = Q.act(lambda e: e.activation(dst[64:128, i0:i0 + 2, 0:255], ps[64:128, :, 1:256], ACT.Copy), op)
                    ops = [o1, o2]
                else:
                    ops = [Q.act(lambda e: e.activation(dst[:, i0:i0 + 2, :], ps, ACT.Copy), op)]
                pair.free = ops
                got[f"t{i0}{shifted}"] = ops
                yield
            return job

        def job_compress(kind):
            def job(pair, w, s):
                zr = yield from have(got, f"t{2 * kind}True")
                zero = Q.dve(lambda e: e.memset(consts[:, 2:3], 0.0)) if False else None
                for m in range(16):
                    z = Z[:, 2 * kind:2 * kind + 2, 2 * m:2 * m + 225:16]
                    wt = w1c[:, kind, 64 * m:64 * m + 64]
                    Q.pe(lambda e, m=m, z=z, wt=wt: e.matmul(
                        pair.t[0:64, 0:30].rearrange("p (g i) -> p g i", g=2), wt, z, start=m == 0, stop=m == 15),
                        zr, ld_e, pair.free)
                for m in range(16):
                    wt = w1c[:, kind, 64 * m:64 * m + 64]
                    pos = CP[:, (POSV if kind else POSK) + m:(POSV if kind else POSK) + m + 1]
                    op = Q.pe(lambda e, m=m, pos=pos, wt=wt: e.matmul(
                        pair.t[0:64, 512:513], wt, pos, start=m == 0, stop=m == 15))
                yield
                x, u, v = w[0][0:64, 0:30], w[0][0:64, 32:62], w[0][0:64, 64:94]
                bias = w[0][0:64, 96:97]
                o = Q.dve(lambda e: e.tensor_copy(bias, pair.t[0:64, 512:513]), op)
                o = Q.dve(lambda e: e.tensor_scalar(x, pair.t[0:64, 0:30], bias, None, ALU.add), o)
                o = Q.dve(lambda e: e.tensor_tensor(u, x, x, ALU.mult), o)
                o = Q.dve(lambda e: e.tensor_tensor(u, u, x, ALU.mult), o)
                o = Q.dve(lambda e: e.scalar_tensor_tensor(out=u, in0=u, scalar=0.044715, in1=x,
                                                           op0=ALU.mult, op1=ALU.add), o)
                k = -2.0 * (2.0 / np.pi) ** 0.5
                o = Q.dve(lambda e: e.tensor_scalar(u, u, float(k), 80.0, ALU.mult, ALU.min), o)
                o = Q.act(lambda e: e.activation(u, u, ACT.Exp), o)
                o = Q.dve(lambda e: e.tensor_scalar(u, u, 1.0, None, ALU.add), o)
                o = Q.dve(lambda e: e.reciprocal(v, u), o)
                o = Q.dve(lambda e: e.tensor_tensor(x, x, v, ALU.mult), o)
                yield
                if kind == 0:
                    op = Q.pe(lambda e: e.matmul(pair.t[:, 0:30], w2c[:, 0:128], x, start=True, stop=True), o)
                    yield
                    o = Q.dve(lambda e: e.tensor_copy(CK[:, 0:30], pair.t[:, 0:30]), op)
                else:
                    for g in range(2):
                        op = Q.pe(lambda e, g=g: e.matmul(pair.t[0:15, 64 * g:64 * g + 64], x[:, 15 * g:15 * g + 15],
                                                          w2c[:, 128:192], start=True, stop=True), o)
                    yield
                    o = Q.dve(lambda e: e.tensor_copy(CK[0:15, 64:192], pair.t[0:15, 0:128]), op)
                pair.free = [o]
                got[f"ck{kind}"] = [o]
                yield
            return job

        gates = small(48)
        acc_n = {}

        def job_nsa(branch, g, t):
            def job(pair, w, s):
                qt = yield from have(got, "qt", 2)
                qs = [QT[64 * (i % 2):64 * (i % 2) + 64, 2 * g + i // 2, 128 * t:128 * t + 128] for i in range(4)]
                if branch == 0:
                    wk = yield from have(got, "ck0")
                    wv = yield from have(got, "ck1")
                    nk, stride = 15, 16
                    ks = [CK[64 * (i % 2):64 * (i % 2) + 64, 15 * g:15 * g + 15] for i in range(4)]
                    mask = CN[:, C_CMP + 16 * t:C_CMP + 16 * t + 15]
                    vs = [[CK[0:15, 64 + 64 * g:128 + 64 * g]] for i in range(4)]
                else:
                    i0 = 0 if branch == 1 else 2
                    wk = yield from have(got, f"t{i0}False")
                    nk = 128 * (t + 1)
                    stride = nk
                    ks = [KT[64 * (i % 2):64 * (i % 2) + 64, i0 + g, 0:nk] for i in range(4)]
                    mask = CN[:, C_CM + 256 - nk:C_CM + 256]
                    va = (N5 + 384 if branch == 1 else N6 + 128) + 64 * g
                    wv = got["b5"] if branch == 1 else got["b6"]
                    vs = [[PJ[:, b, va:va + 64] for b in range(t + 1)] for i in range(4)]
                mask = mask.unsqueeze(1).to_broadcast([128, 4, nk])
                S, rs, ex, rc = yield from softmax4(pair, w, t, qs, ks, mask, 0.125, nk, stride, [qt, wk][0] + list(wk))
                gw = yield from have(got, "gates")
                op = yield from weigh(pair, w, S, nk, vs, 64, ex, list(wv))
                gr = small(4)
                m = Q.dve(lambda e: e.tensor_tensor(gr, rs, gates[:, 24 * t + 8 * branch + 4 * g:24 * t + 8 * branch + 4 * g + 4],
                                                    ALU.mult), rc, gw)
                acc = MX[:, t, 512 + 256 * g:768 + 256 * g].rearrange("p (h c) -> p h c", h=4)
                ps = pair.t[:, 0:256].rearrange("p (h c) -> p h c", h=4)
                gb = gr.unsqueeze(2).to_broadcast([128, 4, 64])
                prev = acc_n.get((g, t))
                if prev is None:
                    o = Q.dve(lambda e: e.tensor_tensor(acc, ps, gb, ALU.mult), m, op)
                    pair.free = [o]
                else:
                    tmp = w[2][:, 0:256].rearrange("p (h c) -> p h c", h=4)
                    q = Q.dve(lambda e: e.tensor_tensor(tmp, ps, gb, ALU.mult), m, op)
                    o = Q.dve(lambda e: e.tensor_tensor(acc, acc, tmp, ALU.add), q, prev)
                    pair.free = [o]
                acc_n[(g, t)] = o
                got.setdefault(f"nsa{t}", []).append(o)
                yield
            return job

        def job_ret(hp):
            def job(pair, w, s):
                rq = yield from have(got, "rq")
                rk = yield from have(got, "rk")
                for i in range(2):
                    for q in range(2):
                        for t in range(2):
                            at = (RK if q else RQ) + 128 * (2 * hp + i)
                            op = Q.pe(lambda e, i=i, q=q, t=t, at=at: e.transpose(
                                pair.t[:, 512 * i + 256 * q + 128 * t:512 * i + 256 * q + 128 * t + 128],
                                PJ[:, t, at:at + 128], ident), rq, rk, pair.free)
                yield
                o1 = Q.act(lambda e: e.activation(w[0][:, 0:512], pair.t[:, 0:512], ACT.Copy), op)
                o2 = Q.dve(lambda e: e.tensor_copy(w[0][:, 512:1024], pair.t[:, 512:1024]), op)
                yield
                for i in range(2):
                    b = 512 * i
                    Q.pe(lambda e, b=b: e.matmul(pair.t[:, b:b + 256], w[0][:, b + 256:b + 384], w[0][:, b:b + 256],
                                                 start=True, stop=True), o1, o2)
                    op = Q.pe(lambda e, b=b: e.matmul(pair.t[:, b + 256:b + 384], w[0][:, b + 384:b + 512],
                                                      w[0][:, b + 128:b + 256], start=True, stop=True))
                yield
                ms = []
                for i in range(2):
                    b, r = 512 * i, 256 * (2 * hp + i)
                    ms.append(Q.dve(lambda e, b=b, r=r: e.tensor_tensor(
                        w[1][:, b:b + 256], pair.t[:, b:b + 256], LC[:, r:r + 256], ALU.mult), op, ld_ret))
                    ms.append(Q.dve(lambda e, b=b, r=r: e.tensor_tensor(
                        w[1][:, b + 256:b + 384], pair.t[:, b + 256:b + 384], LC[:, r:r + 128], ALU.mult)))
                yield
                rv = yield from have(got, "rv")
                for i in range(2):
                    b, v = 512 * i, RV + 128 * (2 * hp + i)
                    Q.pe(lambda e, b=b, v=v: e.matmul(pair.t[:, b:b + 128], w[1][:, b:b + 128], PJ[:, 0, v:v + 128],
                                                      start=True, stop=True), ms, rv)
                    Q.pe(lambda e, b=b, v=v: e.matmul(pair.t[:, b + 128:b + 256], w[1][:, b + 128:b + 256],
                                                      PJ[:, 0, v:v + 128], start=True, stop=False))
                    op = Q.pe(lambda e, b=b, v=v: e.matmul(pair.t[:, b + 128:b + 256], w[1][:, b + 256:b + 384],
                                                           PJ[:, 1, v:v + 128], start=False, stop=True))
                yield
                rg = yield from have(got, "rg")
                st, mv = small(24), small(8)
                va = small(4)
                ags = []
                for i in range(2):
                    for t in range(2):
                        j = 2 * i + t
                        ps = pair.t[:, 512 * i + 128 * t:512 * i + 128 * t + 128]
                        o = Q.dve(lambda e, j=j, ps=ps: e.bn_stats(st[:, 6 * j:6 * j + 6], ps), op)
                        ags.append(Q.dve(lambda e, j=j: e.bn_aggr(mv[:, 2 * j:2 * j + 2], st[:, 6 * j:6 * j + 6]), o))
                o = Q.dve(lambda e: e.tensor_copy(va, mv[:, 1:8:2]), ags)
                r, ro = rstd_of(va, 1, 1.0, o)
                fin = []
                for i in range(2):
                    for t in range(2):
                        j = 2 * i + t
                        c = 128 * (2 * hp + i)
                        ps = pair.t[:, 512 * i + 128 * t:512 * i + 128 * t + 128]
                        tmp = w[2][:, 128 * j:128 * j + 128]
                        o = Q.dve(lambda e, j=j, ps=ps, tmp=tmp: e.tensor_scalar(
                            tmp, ps, mv[:, 2 * j:2 * j + 1], r[:, j:j + 1], ALU.subtract, ALU.mult), ro)
                        fin.append(Q.dve(lambda e, t=t, c=c, tmp=tmp: e.tensor_tensor(
                            MX[:, t, c:c + 128], tmp, PJ[:, t, RG + c:RG + c + 128], ALU.mult), o, rg))
                        got.setdefault(f"ret{t}", []).append(fin[-1])
                pair.free = fin
                yield
            return job

        def e_block(key, at, width):
            pair, op = product_block(xh, xl, nxt, 4)
            got[key] = evacuate(pair, op, at, width, rms)

        e_block("nq", NQ, 512)
        jobs.extend([job_qt(0), job_qt(1)])
        e_block("b5", N5, 512)
        jobs.append(job_twice("b5", N5, Z, 0, True))
        jobs.append(job_twice("b5", N5 + 128, Z, 2, True))
        jobs.append(job_twice("b5", N5 + 256, KT, 0, False))
        jobs.extend([job_compress(0), job_compress(1)])
        e_block("b6", N6, 280)
        jobs.append(job_twice("b6", N6, KT, 2, False))
        got["gates"] = [sigmoid(gates[:, 24 * t:24 * t + 24], PJ[:, t, N6 + 256:N6 + 280], got["b6"][t]) for t in range(2)]
        for br in range(3):
            for t in range(2):
                for g in range(2):
                    jobs.append(job_nsa(br, g, t))
        e_block("rq_", RQ, 512)
        got["rq"] = [rotate(t, RQ, 4, 64, C_RC, C_RS, got["rq_"][t]) for t in range(2)]
        e_block("rk_", RK, 512)
        got["rk"] = [rotate(t, RK, 4, 64, C_RC, C_RS, got["rk_"][t], got["rq"]) for t in range(2)]
        jobs.extend([job_ret(0), job_ret(1)])
        e_block("rv", RV, 512)
        e_block("rg_", RG, 512)
        got["rg"] = []
        for t in range(2):
            rg = PJ[:, t, RG:RG + 512]
            tmp = MSQ[t][:, :]
            o = sigmoid(tmp, rg, got["rg_"][t])
            got["rg"].append(Q.dve(lambda e, rg=rg, tmp=tmp: e.tensor_tensor(rg, rg, tmp, ALU.mult), o))
        mixed = {}
        guard = 0
        while len(got.get("ret0", ())) < 4 or len(got.get("ret1", ())) < 4:
            tick()
        for t in range(2):
            jobs.append(turn_over(MX[:, t, 0:512], t, 0, 4, mh, ml, mixed, got[f"ret{t}"]))
        while len(got["nsa0"]) < 6 or len(got["nsa1"]) < 6:
            tick()
        for t in range(2):
            jobs.append(turn_over(MX[:, t, 512:1024], t, 4, 4, mh, ml, mixed, got[f"nsa{t}"]))
        last_ret = list(got["ret0"]) + list(got["ret1"])
        Q.dma("gpsimd", s_h, LC[:, 0:2176], a["hg"], last_ret)
        nxt, rms = out_rms(mh, ml, mixed, 4, GF0)
        hid = feed_forward(nxt, rms)
        nxt, rms = out_rms(hh, hl, hid, 4, GM1)

        ffn_done = rms.ops[0] + rms.ops[1]
        Q.dma("gpsimd", s_h, HN[:, 0:D], a["lbl"].partition_broadcast(128), ffn_done)
        ld_h = Q.dma("gpsimd", s_h, HN[:, D:D + 128], a["hng"].partition_broadcast(128), ffn_done)
        wr = Q.dve(lambda e: e.tensor_copy(Wr[:, :], LC[:, 0:1152]), ld_h)
        lb, lt = HN[:, 0:D], GB[:, 1, :]
        o = Q.dve(lambda e: e.tensor_tensor(lt, lb, lb, ALU.subtract), ld_h)
        o = Q.act(lambda e: e.activation(lt, lt, ACT.Exp), o)
        o = Q.dve(lambda e: e.tensor_tensor(lb, lt, lt, ALU.subtract), o)
        lb_op = Q.dve(lambda e: e.tensor_scalar(lb, lb, 0.0, None, ALU.max), o)
        HW = {"w": wr}
        hgot = {}
        hfree = [[], []]

        def job_forget(u):
            def job(pair, w, s):
                first = Q.pe(lambda e: e.transpose(pair.t[:, 0:128], ident, ident), pair.free)
                prior = hgot.get(("done", u - 2))
                b = 1024 * (u % 3)
                if u >= 2:
                    yield from have(hgot, ("done", u - 2), 2)
                fin = []
                for t in range(2):
                    fq, ff = PJ[:, t, b:b + 256], PJ[:, t, b + 256:b + 512]
                    gg = PJ[:, t, b + 768:b + 1024]
                    cols = slice(256 * u, 256 * u + 256)
                    lc = slice(256 * (u % 2), 256 * (u % 2) + 256)
                    at = 512 * t
                    L, m, z = w[0][:, at:at + 256], w[1][:, at:at + 256], w[2][:, at:at + 256]
                    y, q_ = w[0][:, at + 256:at + 512], w[1][:, at + 256:at + 512]
                    evf = hgot[("qf", u)][t]
                    o = Q.act(lambda e: e.activation(L, ff, ACT.Abs), first, evf)
                    o = Q.act(lambda e: e.activation(L, L, ACT.Exp, scale=-1.0), o)
                    oL = Q.act(lambda e, L=L: e.activation(L, L, ACT.Ln, bias=1.0), o)
                    o = Q.dve(lambda e, m=m, ff=ff: e.tensor_scalar(m, ff, -1.0, 40.0, ALU.mult, ALU.min), first, evf)
                    o = Q.act(lambda e, m=m: e.activation(m, m, ACT.Exp), o)
                    o = Q.dve(lambda e, m=m, cols=cols: e.tensor_tensor(m, m, lb[:, cols], ALU.mult), o, lb_op)
                    o2 = Q.act(lambda e, m=m: e.activation(m, m, ACT.Ln, bias=1.0), o)
                    o = Q.dve(lambda e, z=z, ff=ff, L=L: e.scalar_tensor_tensor(
                        out=z, in0=ff, scalar=0.0, in1=L, op0=ALU.min, op1=ALU.subtract), oL)
                    o = Q.dve(lambda e, z=z, m=m: e.tensor_tensor(z, z, m, ALU.add), o, o2)
                    h_ = Q.act(lambda e: e.activation(lfh[:, t, lc], z, ACT.Copy), o, prior)
                    l_ = Q.dve(lambda e: e.tensor_tensor(lfl[:, t, lc], z, lfh[:, t, lc].bitcast(F), ALU.subtract), h_)
                    o = Q.dve(lambda e, y=y, ff=ff, L=L: e.scalar_tensor_tensor(
                        out=y, in0=ff, scalar=0.0, in1=L, op0=ALU.max, op1=ALU.add), oL)
                    o = Q.act(lambda e, y=y: e.activation(y, y, ACT.Exp, scale=-1.0), o)
                    p = Q.dve(lambda e, m=m, cols=cols: e.tensor_scalar(m, lb[:, cols], -1.0, 1.0, ALU.mult, ALU.add), l_)
                    k_ = Q.dve(lambda e, y=y, m=m, ff=ff: e.tensor_tensor(ff, y, m, ALU.mult), o, p)
                    o = sigmoid(q_, fq, first, evf)
                    sc = 128 ** -0.5
                    qq = Q.dve(lambda e, fq=fq, q_=q_: e.scalar_tensor_tensor(
                        out=fq, in0=fq, scalar=sc, in1=q_, op0=ALU.mult, op1=ALU.mult), o)
                    fin += [l_, k_, qq]
                    yield
                hgot[("in", u)] = list(fin)
                yield
                yield from have(hgot, ("ig", u), 2)
                for t in range(2):
                    gg = PJ[:, t, b + 768:b + 1024]
                    z = w[2][:, 512 + 256 * t:768 + 256 * t]
                    o = sigmoid(z, gg, first, hgot[("ig", u)][t])
                    ng = HN[:, D:D + 128].unsqueeze(1).to_broadcast([128, 2, 128])
                    o = Q.dve(lambda e, z=z, gg=gg, ng=ng: e.tensor_tensor(
                        gg.rearrange("p (h c) -> p h c", h=2), z.rearrange("p (h c) -> p h c", h=2), ng, ALU.mult),
                        o, ld_h)
                    fin.append(o)
                    hgot.setdefault(("g", u), []).append(o)
                pair.free = fin
                yield
            return job

        def job_head(h):
            def job(pair, w, s):
                u, i = h // 2, h % 2
                ub = 1024 * (u % 3)
                b = ub + 128 * i
                inp = yield from have(hgot, ("in", u), 6)
                T = HQ[s]
                for q in range(2):
                    for t in range(2):
                        op = Q.pe(lambda e, q=q, t=t: e.transpose(
                            pair.t[:, 256 * q + 128 * t:256 * q + 128 * t + 128],
                            PJ[:, t, b + 256 * q:b + 256 * q + 128], ident), inp, pair.free)
                yield
                cp = Q.act(lambda e: e.activation(T[:, 0:512], pair.t[:, 0:512], ACT.Copy), op)
                hc = slice(128 * h, 128 * h + 128)
                lh = slice(256 * (u % 2) + 128 * i, 256 * (u % 2) + 128 * i + 128)
                KX = T[:, 512:640]
                kx_op = None
                fin = []
                busy = [cp]
                for t in range(2):
                    qT = T[:, 128 * t:128 * t + 128]
                    kT = T[:, 256 + 128 * t:256 + 128 * t + 128]
                    yield
                    for part, l in enumerate((lfh, lfl)):
                        for c0, c1, o0 in ((0, 512, 0), (512, 896, 512), (896 + 128 * t, 1024 + 128 * t, 896)):
                            op = Q.pe(lambda e, l=l, c0=c0, c1=c1, o0=o0, part=part: e.matmul(
                                pair.t[:, o0:o0 + c1 - c0], l[:, t, lh], Wr[:, c0:c1],
                                start=part == 0 and o0 % 512 == 0, stop=part == 1, skip_group_check=True), busy, HW["w"])
                    yield
                    ex = Q.act(lambda e: e.activation(w[0][:, :], pair.t[:, :], ACT.Exp), op)
                    gv = w[0][:, 0:896 + 128 * t].rearrange("p (l c) -> p l c", c=128)
                    nq = 7 + t
                    qo = Q.dve(lambda e, gv=gv, nq=nq, qT=qT: e.tensor_tensor(
                        w[1][:, 0:128 * nq].rearrange("p (l c) -> p l c", c=128), gv,
                        qT.unsqueeze(1).to_broadcast([128, nq, 128]), ALU.mult), ex, cp)
                    g7 = w[0][:, 0:896].rearrange("p (l c) -> p l c", c=128)
                    ko = Q.dve(lambda e, g7=g7, kT=kT: e.tensor_tensor(
                        g7, g7, kT.unsqueeze(1).to_broadcast([128, 7, 128]), ALU.mult), qo)
                    if t == 0:
                        kx_op = Q.dve(lambda e, kT=kT: e.tensor_tensor(KX, w[0][:, 896:1024], kT, ALU.mult), ex)
                    yield
                    for l in range(7):
                        Q.pe(lambda e, l=l: e.matmul(pair.t[:, 128 * l:128 * l + 128], w[0][:, 128 * l:128 * l + 128],
                                                     w[1][:, 128 * l:128 * l + 128], start=True, stop=True), ko)
                    op = Q.pe(lambda e, qT=qT, kT=kT: e.matmul(pair.t[:, 896:1024], kT, qT, start=True, stop=True))
                    yield
                    mo = Q.dve(lambda e: e.tensor_tensor(w[2][:, :], pair.t[:, :], LC[:, 1152:2176], ALU.mult), op)
                    AT = T[:, 640:768]
                    ao = Q.dve(lambda e, AT=AT: e.tensor_reduce(
                        AT, w[2][:, :].rearrange("p (l c) -> p c l", c=128), X_AX, ALU.add), mo)
                    v0 = PJ[:, 0, ub + 512 + 128 * i:ub + 640 + 128 * i]
                    v1 = PJ[:, 1, ub + 512 + 128 * i:ub + 640 + 128 * i]
                    ig = yield from have(hgot, ("ig", u), 2)
                    axo = None
                    if t == 1:
                        yield
                        op = Q.pe(lambda e: e.matmul(pair.t[:, 0:128], KX, w[1][:, 896:1024], start=True, stop=True),
                                  mo, kx_op)
                        axo = Q.act(lambda e: e.activation(w[0][:, 0:128], pair.t[:, 0:128], ACT.Copy), op)
                    yield
                    op = Q.pe(lambda e, AT=AT, t=t: e.matmul(pair.t[:, 512:640], AT, v1 if t else v0,
                                                             start=True, stop=t == 0), ao, ig)
                    if t == 1:
                        op = Q.pe(lambda e: e.matmul(pair.t[:, 512:640], w[0][:, 0:128], v0, start=False, stop=True), axo)
                    yield
                    ms = small(1)
                    so = Q.act(lambda e, ms=ms: e.activation(w[2][:, 0:128], pair.t[:, 512:640], ACT.Square,
                                                             accum_out=ms), op)
                    r, ro = rstd_of(ms, 0, 1.0 / 128, so)
                    go = yield from have(hgot, ("g", u), 2)
                    gs = PJ[:, t, ub + 768 + 128 * i:ub + 896 + 128 * i]
                    fo = Q.dve(lambda e, t=t, r=r, gs=gs: e.scalar_tensor_tensor(
                        out=MX[:, t, hc], in0=pair.t[:, 512:640], scalar=r, in1=gs, op0=ALU.mult, op1=ALU.mult), ro, go)
                    busy = [fo, ao, mo]
                    fin.append(fo)
                    hgot.setdefault(("mx", t, h // 4), []).append(fo)
                pair.free = fin
                hgot.setdefault(("done", u), []).extend([fin[-1]])
                yield
            return job

        def until2(store, key, n):
            while len(store.get(key, ())) < n:
                tick()
            return store[key]

        for u in range(4):
            pair, op = product_block(xh, xl, nxt, 4)
            over = until2(hgot, ("done", u - 3), 2) if u >= 3 else None
            hgot[("qf", u)] = evacuate(pair, op, 1024 * (u % 3), 512, rms, over)
            jobs.append(job_forget(u))
            pair, op = product_block(xh, xl, nxt, 4)
            hgot[("ig", u)] = evacuate(pair, op, 1024 * (u % 3) + 512, 512, rms, over)
            jobs.extend([job_head(2 * u), job_head(2 * u + 1)])
        mixed = {}
        for half in range(2):
            for t in range(2):
                while len(hgot.get(("mx", t, half), ())) < 4:
                    tick()
            for t in range(2):
                jobs.append(turn_over(MX[:, t, 512 * half:512 * half + 512], t, 4 * half, 4, mh, ml, mixed,
                                      hgot[("mx", t, half)]))
        hg_done = [x for k, v in hgot.items() if k[0] == "mx" for x in v]
        gb = load_gb(a["fng"])
        nxt, rms = out_rms(mh, ml, mixed, 4, GF1)
        hid = feed_forward(nxt, rms)
        nxt, rms = out_rms(hh, hl, hid, 4, None)
        drain()
        nxt = {}
        fin = []
        for t in range(2):
            x = X[:, t, :]
            fin.append(Q.dve(lambda e, x=x, t=t: e.scalar_tensor_tensor(
                out=x, in0=x, scalar=rms.r[t][0], in1=GB[:, 0, :], op0=ALU.mult, op1=ALU.mult),
                rms.r[t][1], gb, rms.ops[t]))
            jobs.append(turn_over(x, t, 0, 8, xh, xl, nxt, [fin[t]]))
        gb_use[0] = fin

        Q.dma("gpsimd", s_a, AG[:, 0:128], a["asg"].partition_broadcast(128), fin)
        ld_a = Q.dma("gpsimd", s_a, AG[:, 128:384], a["alam"].partition_broadcast(128), fin)
        lam = small(8)
        los = []
        for i in range(2):
            los.append(Q.dve(lambda e, i=i: e.tensor_tensor(AG[:, 128 + 128 * i:192 + 128 * i], AG[:, 128 + 128 * i:192 + 128 * i],
                                                            AG[:, 192 + 128 * i:256 + 128 * i], ALU.mult), ld_a))
            los.append(Q.dve(lambda e, i=i: e.tensor_reduce(lam[:, i:i + 1], AG[:, 128 + 128 * i:192 + 128 * i],
                                                            X_AX, ALU.add), los[-1]))
        o = Q.act(lambda e: e.activation(lam[:, 2:4], lam[:, 0:2], ACT.Exp), los)
        o = Q.dve(lambda e: e.tensor_tensor(lam[:, 4:5], lam[:, 2:3], lam[:, 3:4], ALU.subtract), o)
        lam_op = Q.dve(lambda e: e.tensor_scalar(lam[:, 5:6], lam[:, 4:5], LAM0, None, ALU.add), o)
        ag_op = Q.dve(lambda e: e.tensor_scalar(AG[:, 0:128], AG[:, 0:128], 1.0 - LAM0, None, ALU.mult), ld_a)

        agot = {}

        def job_turn(key, qat, kat, i0, n, extra):
            def job(pair, w, s):
                for t in range(2):
                    for q in range(2):
                        for i in range(n):
                            at = (kat if q else qat) + 128 * i
                            op = Q.pe(lambda e, q=q, i=i, t=t, at=at: e.transpose(
                                pair.t[:, (q * n + i) * 256 + 128 * t:(q * n + i) * 256 + 128 * t + 128],
                                PJ[:, t, at:at + 128], ident), extra[t], pair.free)
                yield
                half = 256 * n
                o1 = Q.act(lambda e: e.activation(QTa[:, i0:i0 + n, :], pair.t[:, 0:half].rearrange(
                    "p (i c) -> p i c", i=n), ACT.Copy), op)
                o2 = Q.dve(lambda e: e.tensor_copy(KTa[:, i0:i0 + n, :], pair.t[:, half:2 * half].rearrange(
                    "p (i c) -> p i c", i=n)), op)
                pair.free = [o1, o2]
                agot[key] = [o1, o2]
                yield
            return job

        def job_diff(p, t, vat, vkey):
            def job(pair, w, s):
                kq = yield from have(agot, ("qk", p))
                nk = 128 * (t + 1)
                qs = [QTa[64 * (i % 2):64 * (i % 2) + 64, 2 * p + i // 2, 128 * t:128 * t + 128] for i in range(4)]
                ks = [KTa[64 * (i % 2):64 * (i % 2) + 64, 2 * p + i // 2, 0:nk] for i in range(4)]
                mask = CN[:, C_KM + 256 - nk:C_KM + 256].unsqueeze(1).to_broadcast([128, 4, nk])
                S, rs, ex, rc = yield from softmax4(pair, w, t, qs, ks, mask, 0.125, nk, nk, kq)
                rl = small(2)
                lo = Q.dve(lambda e: e.tensor_scalar(rl, rs[:, 1:4:2], lam[:, 5:6], None, ALU.mult), rc, lam_op)
                cs = []
                for i in range(2):
                    d = w[2][:, nk * i:nk * i + nk]
                    o = Q.dve(lambda e, i=i, d=d: e.tensor_scalar(d, S[:, 2 * i + 1, :], rl[:, i:i + 1], None, ALU.mult), lo)
                    cs.append(Q.dve(lambda e, i=i, d=d: e.scalar_tensor_tensor(
                        out=d, in0=S[:, 2 * i, :], scalar=rs[:, 2 * i:2 * i + 1], in1=d, op0=ALU.mult, op1=ALU.subtract), o))
                yield
                vo = yield from have(agot, vkey, 2)
                C2 = w[2][:, 0:2 * nk].rearrange("p (h k) -> p h k", h=2)
                vs = [[PJ[:, b, vat + 128 * i:vat + 128 * i + 128] for b in range(t + 1)] for i in range(2)]
                op = yield from weigh(pair, w, C2, nk, vs, 128, cs, list(vo), n=2)
                ms = small(2)
                sq = [Q.act(lambda e, i=i: e.activation(w[0][:, 128 * i:128 * i + 128], pair.t[:, 128 * i:128 * i + 128],
                                                        ACT.Square, accum_out=ms[:, i:i + 1]), op) for i in range(2)]
                r, ro = rstd_of(ms, 1, 1.0 / 128, sq)
                fin = []
                for i in range(2):
                    c = 128 * (2 * p + i)
                    fin.append(Q.dve(lambda e, i=i, c=c: e.scalar_tensor_tensor(
                        out=MX[:, t, c:c + 128], in0=pair.t[:, 128 * i:128 * i + 128], scalar=r[:, i:i + 1],
                        in1=AG[:, 0:128], op0=ALU.mult, op1=ALU.mult), ro, ag_op, agot["rot"]))
                agot.setdefault(("mx", t, p // 2), []).extend(fin)
                pair.free = fin
                yield
            return job

        agot["rot"] = []
        gb = load_gb(a["lng"][0:D], a["lnb"][0:D])

        def rotate_a(t, at, *waits):
            x = PJ[:, t, at:at + 512].rearrange("p (h c) -> p h c", h=8)
            y = MSQ[t][:, :].rearrange("p (h c) -> p h c", h=8)
            co = CN[:, C_AC + 64 * t:C_AC + 64 * t + 64].unsqueeze(1).to_broadcast([128, 8, 64])
            s0 = CN[:, C_AS + 64 * t:C_AS + 64 * t + 32].unsqueeze(1).to_broadcast([128, 8, 32])
            s1 = CN[:, C_AS + 64 * t + 32:C_AS + 64 * t + 64].unsqueeze(1).to_broadcast([128, 8, 32])
            p = Q.dve(lambda e: e.tensor_tensor(y[:, :, 0:32], x[:, :, 32:64], s0, ALU.mult), *waits)
            p = Q.dve(lambda e: e.tensor_tensor(y[:, :, 32:64], x[:, :, 0:32], s1, ALU.mult), p)
            q = Q.dve(lambda e: e.tensor_tensor(x, x, co, ALU.mult), p)
            return Q.dve(lambda e: e.tensor_tensor(x, x, y, ALU.add), q)

        def a_block(at):
            pair, op = product_block(xh, xl, nxt, 4)
            return evacuate(pair, op, at, 512, None)

        def qk_block(p, at, rot):
            ev = a_block(at)
            if rot:
                ev = [rotate_a(t, at, ev[t]) for t in range(2)]
            jobs.append(job_turn(("qk", p), at, at + 256, 2 * p, 2, ev))

        for v in range(2):
            b = 1536 * v
            qk_block(2 * v, b, True)
            agot[("v", v)] = a_block(b + 512)
            for t in range(2):
                jobs.append(job_diff(2 * v, t, b + 512, ("v", v)))
            qk_block(2 * v + 1, b + 1024, True)
            for t in range(2):
                jobs.append(job_diff(2 * v + 1, t, b + 768, ("v", v)))

        def mix_over(store, n):
            mixed = {}
            for half in range(2):
                for t in range(2):
                    while len(store.get(("mx", t, half), ())) < n:
                        tick()
                for t in range(2):
                    jobs.append(turn_over(MX[:, t, 512 * half:512 * half + 512], t, 4 * half, 4, mh, ml, mixed,
                                          store[("mx", t, half)]))
            return mixed

        mixed = mix_over(agot, 4)
        nxt, _ = out_ln(mh, ml, mixed, 4, gb)
        gb = load_gb(a["lng"][D:2 * D], a["lnb"][D:2 * D])
        hid = feed_forward(nxt, None)
        nxt, fin = out_ln(hh, hl, hid, 4, gb)
        gb = load_gb(a["lng"][2 * D:3 * D], a["lnb"][2 * D:3 * D])

        agot.clear()

        def job_band(p, t, vat, vkey):
            def job(pair, w, s):
                kq = yield from have(agot, ("qk", p))
                nk = 128 * (t + 1)
                qs = [QTa[64 * (i % 2):64 * (i % 2) + 64, 2 * p + i // 2, 128 * t:128 * t + 128] for i in range(4)]
                ks = [KTa[64 * (i % 2):64 * (i % 2) + 64, 2 * p + i // 2, 0:nk] for i in range(4)]
                tb_op = agot[("tb", p)]
                mask = TB[p % 2][:, :].rearrange("p (h k) -> p h k", h=4)[:, :, 256 - nk:256]
                S, rs, ex, rc = yield from softmax4(pair, w, t, qs, ks, mask, 0.125, nk, nk, kq, tb_op)
                agot.setdefault(("used", p), []).extend(ex[-1:])
                vo = yield from have(agot, vkey, 2)
                vs = [[PJ[:, b, vat + 64 * i:vat + 64 * i + 64] for b in range(t + 1)] for i in range(4)]
                op = yield from weigh(pair, w, S, nk, vs, 64, ex, list(vo))
                o = Q.dve(lambda e: e.tensor_tensor(
                    MX[:, t, 256 * p:256 * p + 256].rearrange("p (h c) -> p h c", h=4),
                    pair.t[:, 0:256].rearrange("p (h c) -> p h c", h=4),
                    rs.unsqueeze(2).to_broadcast([128, 4, 64]), ALU.mult), rc, op)
                agot.setdefault(("mx", t, p // 2), []).append(o)
                pair.free = [o]
                yield
            return job

        km = CN[:, C_KM:C_KM + 256].unsqueeze(1).to_broadcast([128, 4, 256])
        s_tb = [[sem(f"d_tb{i}"), 0] for i in range(2)]

        def load_bias(p, *waits):
            ld = Q.dma("gpsimd", s_tb[p % 2], TB[p % 2][:, :], a["rel"][:, 1024 * p:1024 * p + 1024], *waits)
            tb = TB[p % 2][:, :].rearrange("p (h k) -> p h k", h=4)
            agot[("tb", p)] = [Q.pool(lambda e: e.tensor_tensor(tb, tb, km, ALU.add), ld)]

        load_bias(0, fin)
        load_bias(1, fin)
        for v in range(2):
            b = 1536 * v
            if v == 1:
                for p in range(2):
                    load_bias(2 + p, until2(agot, ("used", p), 2))
            qk_block(2 * v, b, False)
            agot[("v", v)] = a_block(b + 512)
            for t in range(2):
                jobs.append(job_band(2 * v, t, b + 512, ("v", v)))
            qk_block(2 * v + 1, b + 1024, False)
            for t in range(2):
                jobs.append(job_band(2 * v + 1, t, b + 768, ("v", v)))
        mixed = mix_over(agot, 2)
        nxt, _ = out_ln(mh, ml, mixed, 4, gb)
        gb = load_gb(a["lng"][3 * D:4 * D], a["lnb"][3 * D:4 * D])
        hid = feed_forward(nxt, None)
        _, fin = out_ln(hh, hl, hid, 4, gb, last=True)
        drain()
        outs = [Q.dma("sync", s_out, out[128 * t:128 * t + 128, :], X[:, t, :], fin[t]) for t in range(2)]
        assert cur[0] == len(stream)

        Q.count(sems)
        block = ctx.enter_context(nc.Block())

        @block.sync
        def _(e):
            Q.emit("sync", e)
            e.wait_ge(s_out[0], outs[-1].value)

        @block.tensor
        def _(e):
            Q.emit("tensor", e)

        @block.vector
        def _(e):
            Q.emit("vector", e)

        @block.scalar
        def _(e):
            Q.emit("scalar", e)

        @block.gpsimd
        def _(e):
            Q.emit("gpsimd", e)


def kernel(**inputs):
    import concourse.bacc as bacc
    from concourse.bass_utils import run_bass_kernel_spmd

    g = {k: np.asarray(v) for k, v in inputs.items()}
    consts, ret, hg = shape_constants()
    col = lambda v: v.reshape(-1, 128).T
    arrays = {
        "x": g["x"][0],
        "consts": consts, "ret": ret, "hg": hg,
        "cols": np.concatenate([col(g["norm_mix_g"][0]), col(g["norm_ffn_g"][0]), col(g["norm_mix_g"][1]),
                                col(g["norm_ffn_g"][1]), col(g["cmp_pos_k"][0].reshape(-1)),
                                col(g["cmp_pos_v"][0].reshape(-1))], 1),
        "cw1k": g["cmp_w1_k"][0].reshape(16, 128, 64).transpose(1, 0, 2).reshape(128, 1024),
        "cw1v": g["cmp_w1_v"][0].reshape(16, 128, 64).transpose(1, 0, 2).reshape(128, 1024),
        "cw2k": g["cmp_w2_k"][0], "cw2v": g["cmp_w2_v"][0],
        "lbl": g["hgrn_lb_logits"][0], "hng": g["hgrn_norm_g"][0], "fng": g["final_norm_g"],
        "asg": g["a_subln_g_2"][0], "alam": g["a_lambda_2"][0].reshape(-1),
        "lng": g["ln_g_2"].reshape(-1), "lnb": g["ln_b_2"].reshape(-1),
    }
    at = 128 - np.arange(128)[:, None] + np.arange(256)[None, :]
    arrays["rel"] = g["b_rel_bias_2"][0][:, at].transpose(1, 0, 2).reshape(128, 4096)
    ffi, ffo = g["ffn_w_in_2"], g["ffn_w_out_2"]
    qkv_b = np.concatenate([g["b_w_q_2"][0], g["kv_w_2"]], 1)
    mats = {
        "w_e": g["even_w_in"][0][:, E_COLS], "w_eo": g["even_w_out"][0],
        "w_h": g["odd_w_in"][0][:, H_COLS], "w_ho": g["odd_w_out"][0],
        "w_a": g["a_w_qkv_2"][0][:, A_COLS], "w_ao": g["a_w_o_2"][0],
        "w_b": qkv_b[:, A_COLS], "w_bo": g["b_w_o_2"][0],
    }
    for i in range(2):
        mats[f"g{i}"], mats[f"u{i}"], mats[f"d{i}"] = g["ffn_w1"][i], g["ffn_w3"][i], g["ffn_w2"][i]
        mats[f"g{i + 2}"], mats[f"u{i + 2}"], mats[f"d{i + 2}"] = ffi[i][:, :FF], ffi[i][:, FF:], ffo[i]
    for name, w in mats.items():
        arrays[name] = lay_out(w, name)
    arrays = {k: np.ascontiguousarray(v) for k, v in arrays.items()}

    nc = bacc.Bacc("TRN2", target_bir_lowering=False, num_devices=1)
    aps = {k: nc.dram_tensor(f"in_{k}", v.shape, mybir.dt.from_np(v.dtype), kind="ExternalInput").ap()
           for k, v in arrays.items()}
    out = nc.dram_tensor("out_0", (256, D), F, kind="ExternalOutput").ap()
    program(nc, aps, out)
    r = run_bass_kernel_spmd(nc, [{f"in_{k}": v for k, v in arrays.items()}], core_ids=[0])
    return r.results[0]["out_0"].reshape(1, 256, D)
```

```python
from collections import deque
from contextlib import ExitStack

import numpy as np

import concourse.bass as bass
from concourse import mybir

ALU = mybir.AluOpType
ACT = mybir.ActivationFunctionType
X_AX = mybir.AxisListType.X
F = mybir.dt.float32
R = mybir.dt.float32r

D = 1024
FF = 2816
NEG = -1.0e30
ALPHA = 4 ** 0.25
LAM0 = 0.8 - 0.6
EPS = 1e-6
LN_EPS = 1e-5

LEVELS = [64, 32, 16, 8, 4, 2, 1]
NLEV = len(LEVELS)

GM0, GF0, GM1, GF1, POSK, POSV = 0, 8, 16, 24, 32, 48
NCOLP = 64
C_ID, C_CM, C_KM, C_CMP, C_RC, C_RS, C_AC, C_AS = 0, 128, 384, 640, 672, 928, 1184, 1312
NCONST = 1440
NSMALL = 960


def ranges(*parts):
    return np.concatenate([np.arange(a, a + n) for a, n in parts])


def blocks_of(width):
    return [min(512, width - c) for c in range(0, width, 512)]


E_COLS = ranges((2048, 512), (2560, 512), (3072, 280), (0, 512), (512, 512), (1024, 512), (1536, 512))
E_BLOCKS = [512, 512, 280, 512, 512, 512, 512]
H_COLS = ranges(*[(a + 256 * u, 256) for u in range(4) for a in (0, 1024, 2048, 3072)])
A_COLS = ranges(*[p for v in range(2) for p in (
    (512 * v, 256), (1024 + 512 * v, 256), (2048 + 512 * v, 512), (512 * v + 256, 256), (1280 + 512 * v, 256))])
WIDE = ("w_eo", "w_ho", "w_ao", "w_bo")
WEIGHTS = {
    "w_e": (D, E_BLOCKS), "w_eo": (D, [512] * 2), "w_h": (D, [512] * 8), "w_ho": (D, [512] * 2),
    "w_a": (D, [512] * 6), "w_ao": (D, [512] * 2), "w_b": (D, [512] * 6), "w_bo": (D, [512] * 2),
    "u0": (D, blocks_of(FF)), "u1": (D, blocks_of(FF)), "u2": (D, blocks_of(FF)), "u3": (D, blocks_of(FF)),
    "g0": (D, blocks_of(FF)), "g1": (D, blocks_of(FF)), "g2": (D, blocks_of(FF)), "g3": (D, blocks_of(FF)),
    "d0": (FF, [512] * 2), "d1": (FF, [512] * 2), "d2": (FF, [512] * 2), "d3": (FF, [512] * 2),
}


def chunks_of(K, width):
    n = K // 128
    per = 1024 // width
    return [(k, min(per, n - k)) for k in range(0, n, per)]


def lay_out(w, name):
    K, blocks = WEIGHTS[name]
    if name in WIDE:
        tiles = w.reshape(4, 2, 128, 2, 512).transpose(0, 3, 2, 1, 4)
        return np.ascontiguousarray(tiles).reshape(-1)
    parts, c = [], 0
    for width in blocks:
        for k, n in chunks_of(K, width):
            tile = w[128 * k:128 * (k + n), c:c + width].reshape(n, 128, width)
            parts.append(np.ascontiguousarray(tile.transpose(1, 0, 2)).reshape(-1))
        c += width
    return np.concatenate(parts)


def shape_constants():
    p = np.arange(128)[:, None]
    c = np.zeros((128, NCONST), np.float32)
    c[:, C_ID:C_ID + 128] = np.eye(128)
    j = np.arange(128)[None, :]
    c[:, C_CM + 128:C_CM + 256] = np.where(j <= p, 0.0, NEG)
    c[:, C_KM + 128:C_KM + 256] = np.where(j // 64 <= p // 64, 0.0, NEG)
    for t in range(2):
        n = np.arange(16)[None, :]
        c[:, C_CMP + 16 * t:C_CMP + 16 * t + 16] = np.where(16 * n + 31 <= 128 * t + p, 0.0, NEG)
    for half, at_c, at_s in ((64, C_RC, C_RS), (32, C_AC, C_AS)):
        inv = (np.float32(10000.0) ** (-np.arange(half, dtype=np.float32) / np.float32(half))).astype(np.float32)
        for t in range(2):
            ang = ((128 * t + np.arange(128, dtype=np.float32))[:, None] * inv[None, :]).astype(np.float32)
            co, si = np.cos(ang.astype(np.float64)), np.sin(ang.astype(np.float64))
            w = 2 * half
            c[:, at_c + w * t:at_c + w * t + w] = np.concatenate([co, co], 1)
            c[:, at_s + w * t:at_s + w * t + w] = np.concatenate([-si, si], 1)
    ret = np.zeros((128, 4, 256), np.float32)
    t = np.arange(256)[None, :]
    for h in range(4):
        lg = np.log(1.0 - 2.0 ** (-5.0 - h))
        ret[:, h] = np.where(t >= p, np.exp(lg * np.maximum(t - p, 0)), 0.0) * 128 ** -0.5
    s = np.arange(128)[:, None]
    n = np.arange(128)[None, :]
    hw = np.zeros((128, 9, 128), np.float32)
    hm = np.zeros((128, 8, 128), np.float32)
    for i, L in enumerate(LEVELS):
        mid = n // (2 * L) * 2 * L + L - 1
        right = n % (2 * L) >= L
        hw[:, i] = np.where(right, (s > mid) & (s <= n), (s > n) & (s <= mid))
        m = s
        hm[:, i] = (m // (2 * L) == n // (2 * L)) & (m % (2 * L) < L) & (n % (2 * L) >= L)
    hw[:, 7] = s > n
    hw[:, 8] = s <= n
    hm[:, 7] = s == n
    return c, ret.reshape(128, 1024), np.concatenate([hw.reshape(128, -1), hm.reshape(128, -1)], 1)


def width(ap):
    n = 1
    for x in ap.shape[1:]:
        n *= x
    return n


def vector_ns(out, rate=1.04):
    return 70 + rate * width(out)


class Calls:

    def matmul(self, out, lhsT, rhs, **k):
        return lambda e: e.matmul(out, lhsT, rhs, **k), max(64, width(rhs)) * (0.42 if rhs.dtype == R else 1.68) + 4

    def transpose(self, *a, **k):
        return lambda e: e.transpose(*a, **k), 110

    def activation(self, out, in_, func, **k):
        return (lambda e: e.activation(out, in_, func, **k),
                190 + 0.833 * width(out) + 95 * ("accum_out" in k) + 95 * ("bias" in k))

    def tensor_tensor(self, out, *a, **k):
        return lambda e: e.tensor_tensor(out, *a, **k), vector_ns(out)

    def tensor_scalar(self, out, *a, **k):
        return lambda e: e.tensor_scalar(out, *a, **k), vector_ns(out, 0.52)

    def scalar_tensor_tensor(self, **k):
        return lambda e: e.scalar_tensor_tensor(**k), vector_ns(k["out"])

    def tensor_reduce(self, out, in_, *a, **k):
        return lambda e: e.tensor_reduce(out, in_, *a, **k), vector_ns(in_)

    def tensor_copy(self, out, *a, **k):
        return lambda e: e.tensor_copy(out, *a, **k), vector_ns(out, 0.8)

    def reciprocal(self, out, *a, **k):
        return lambda e: e.reciprocal(out, *a, **k), vector_ns(out, 6.3)

    def bn_stats(self, out, in_, *a, **k):
        return lambda e: e.bn_stats(out, in_, *a, **k), vector_ns(in_)

    def bn_aggr(self, out, *a, **k):
        return lambda e: e.bn_aggr(out, *a, **k), 80

    def memset(self, *a, **k):
        return lambda e: e.memset(*a, **k), 100

    def preload_act_table_set(self, *a, **k):
        return lambda e: e.preload_act_table_set(*a, **k), 1283

    def dma_start(self, *a, **k):
        return lambda e: e.dma_start(*a, **k), 1400


CALLS = Calls()
HOP = 100


class Op:

    def __init__(self, fn, waits):
        self.fn, self.waits, self.sem, self.value, self.signals, self.t = fn, waits, None, 0, False, 0.0


class Queues:

    def __init__(self):
        self.q = {k: [] for k in ("sync", "tensor", "vector", "scalar", "gpsimd")}
        self.clock = dict.fromkeys(self.q, 0.0)
        self.newest = None

    def add(self, eng, make, *waits):
        fn, cost = make(CALLS)
        flat = []
        for w in waits:
            flat += list(w) if isinstance(w, (list, tuple)) else [w] if w is not None else []
        for w in flat:
            w.signals = True
        op = Op(fn, flat)
        begin = max([self.clock[eng]] + [w.t + HOP for w in flat])
        self.clock[eng] = begin + cost
        op.t = begin + cost + (2000 if eng == "sync" else 0)
        self.newest = max(self.newest or 0.0, op.t)
        self.q[eng].append(op)
        return op

    def pe(self, fn, *w):
        return self.add("tensor", fn, *w)

    def act(self, fn, *w):
        return self.add("scalar", fn, *w)

    def dve(self, fn, *w):
        return self.add("vector", fn, *w)

    def pool(self, fn, *w):
        return self.add("gpsimd", fn, *w)

    def dma(self, eng, sem, out, src, *w):
        op = self.add(eng, lambda e: e.dma_start(out, src), *w)
        sem[1] += 16
        op.sem, op.value = sem[0], sem[1]
        return op

    def count(self, sems):
        for k, ops in self.q.items():
            n = 0
            for op in ops:
                if op.sem is None and op.signals:
                    n += 1
                    op.sem, op.value = sems[k], n

    def emit(self, k, e):
        seen = {}
        for op in self.q[k]:
            for w in op.waits:
                key = w.sem.name
                if seen.get(key, 0) < w.value:
                    e.wait_ge(w.sem, w.value)
                    seen[key] = w.value
            ins = op.fn(e)
            if op.sem is not None:
                ins.then_inc(op.sem, 16 if op.value and k in ("sync", "gpsimd") and op.sem.name.startswith("d_") else 1)


class Pair:

    def __init__(self, tile):
        self.t, self.free = tile, []

    def of_bank(self, t):
        return [op for i, op in enumerate(self.free) if len(self.free) != 2 or i == t]


def program(nc, a, out):
    ctx = ExitStack()
    with ctx:
        def sb(name, shape, dt=F, stack=ctx):
            return stack.enter_context(nc.sbuf_tensor(name, shape, dt))

        def sem(name):
            return ctx.enter_context(nc.semaphore(name))

        Q = Queues()
        NR, NH, LA = 5, 4, 2

        G = [Pair(ctx.enter_context(nc.psum_tensor(f"G{i}", [128, 1024], F))) for i in range(2)]
        A = [Pair(ctx.enter_context(nc.psum_tensor(f"A{i}", [128, 1024], F))) for i in range(2)]

        raw = [sb(f"raw{i}", [128, 1024]) for i in range(NR)]
        whi = [sb(f"whi{i}", [128, 1024], R) for i in range(NH)]
        wlo = [sb(f"wlo{i}", [128, 1024], R) for i in range(NH)]
        X = sb("X", [128, 2, D])
        xh = sb("xh", [128, 8, 256], R)
        xl = sb("xl", [128, 8, 256], R)
        CN = sb("CN", [128, NCONST])
        CP = sb("CP", [128, NCOLP])
        GB = sb("GB", [128, 2, D])
        LC = sb("LC", [128, 2176])
        SM = sb("SM", [128, NSMALL])
        MSQ = [sb(f"MSQ{t}", [128, 512]) for t in range(2)]
        W = [[sb(f"W{s}{i}", [128, 1024]) for i in range(2)] for s in range(3)]

        shared = ExitStack()
        mh = sb("mh", [128, 8, 256], R, shared)
        ml = sb("ml", [128, 8, 256], R, shared)
        MX = sb("MX", [128, 2, D], F, shared)
        PJ = sb("PJ", [128, 2, 3352], F, shared)
        mixer = ExitStack()
        shared.enter_context(mixer)
        e0 = ExitStack()
        QT = sb("QT", [128, 4, 256], F, e0)
        KT = sb("KT", [128, 4, 256], F, e0)
        Z = sb("Z", [128, 4, 256], F, e0)
        w1c = sb("w1c", [128, 2, 16 * 64], F, e0)
        w2c = sb("w2c", [64, 256], F, e0)
        CK = sb("CK", [128, 512], F, e0)
        e0.close()
        e1 = ExitStack()
        lfh = sb("lfh", [128, 2, 512], R, e1)
        lfl = sb("lfl", [128, 2, 512], R, e1)
        Wr = sb("Wr", [128, 9 * 128], R, e1)
        HN = sb("HN", [128, D + 128], F, e1)
        HT = [sb(f"HT{s}", [128, 1024], F, e1) for s in range(2)]
        HX = sb("HX", [128, 4 * 128], F, e1)
        e1.close()
        e2 = ExitStack()
        QTa = sb("QTa", [128, 8, 256], F, e2)
        KTa = sb("KTa", [128, 8, 256], F, e2)
        AG = sb("AG", [128, 384], F, e2)
        TB = [sb(f"TB{s}", [128, 1024], F, e2) for s in range(2)]
        e2.close()
        shared.close()
        ffn = ExitStack()
        hh = sb("hh", [128, 22, 256], R, ffn)
        hl = sb("hl", [128, 22, 256], R, ffn)
        sa = [sb(f"sa{i}", [128, 2, 512], F, ffn) for i in range(2)]
        ffn.close()

        sems = {k: sem(f"s_{k}") for k in Q.q}
        s_raw = [[sem(f"d_raw{i}"), 0] for i in range(NR)]
        s_cn = [sem("d_cn"), 0]
        s_lc = [sem("d_lc"), 0]
        s_e = [sem("d_e"), 0]
        s_gb = [sem("d_gb"), 0]
        s_h = [sem("d_h"), 0]
        s_a = [sem("d_a"), 0]
        s_out = [sem("d_out"), 0]

        used = [0]

        def small(n):
            at = used[0]
            used[0] += n
            assert used[0] <= NSMALL, used
            return SM[:, at:at + n]

        ld_x = Q.dma("sync", [sem("d_x"), 0], X[:, :, :], a["x"].rearrange("(t p) d -> p t d", p=128))
        Q.dma("sync", s_cn, CN[:, :], a["consts"])
        ld_cn = Q.dma("sync", s_cn, CP[:, :], a["cols"])
        ld_ret = Q.dma("gpsimd", s_lc, LC[:, 0:1024], a["ret"])
        Q.dma("gpsimd", s_e, w1c[:, 0, :], a["cw1k"])
        Q.dma("gpsimd", s_e, w1c[:, 1, :], a["cw1v"])
        Q.dma("gpsimd", s_e, w2c[:, 0:64], a["cw2k"])
        Q.dma("gpsimd", s_e, w2c[:, 64:128], a["cw2k"])
        ld_e = Q.dma("gpsimd", s_e, w2c[:, 128:192], a["cw2v"])
        ident = CN[:, C_ID:C_ID + 128]

        def exp_tables():
            Q.act(lambda e: e.preload_act_table_set("natural_log_exp_and_others"))

        exp_tables()
        consts = small(4)
        c_eps = [Q.dve(lambda e: e.memset(consts[:, 0:1], EPS)),
                 Q.dve(lambda e: e.memset(consts[:, 1:2], LN_EPS))]

        stream = []
        order = ["w_e", "w_eo", ("g0", "u0"), "d0", "w_h", "w_ho", ("g1", "u1"), "d1",
                 "w_a", "w_ao", ("g2", "u2"), "d2", "w_b", "w_bo", ("g3", "u3"), "d3"]
        for o in order:
            names = o if isinstance(o, tuple) else (o,)
            at = dict.fromkeys(names, 0)
            K, blocks = WEIGHTS[names[0]]
            if o in WIDE:
                stream += [(o, 131072 * i, i // 2 * 2, 2, 512) for i in range(8)]
                continue
            for width in blocks:
                for name in names:
                    for k, n in chunks_of(K, width):
                        stream.append((name, at[name], k, n, width))
                        at[name] += 128 * n * width
        hi_op, lo_op, pe_op = [], [], []

        def ensure(upto):
            while len(hi_op) <= min(upto, len(stream) - 1):
                c = len(hi_op)
                name, at, _, n, width = stream[c]
                r, h, m = raw[c % NR], c % NH, n * width
                src = a[name][at:at + 128 * m].rearrange("(p m) -> p m", p=128)
                ld = Q.dma("sync", s_raw[c % NR], r[:, 0:m], src, lo_op[c - NR] if c >= NR else None)
                gone = pe_op[c - NH] if c >= NH else None
                hi_op.append(Q.act(lambda e, h=h, r=r, m=m: e.activation(whi[h][:, 0:m], r[:, 0:m], ACT.Copy),
                                   ld, gone))
                lo_op.append(Q.dve(lambda e, h=h, r=r, m=m: e.tensor_tensor(
                    wlo[h][:, 0:m], r[:, 0:m], whi[h][:, 0:m].bitcast(F), ALU.subtract), hi_op[c]))

        jobs = deque()
        running = [None, None, None]
        side = [A[0], A[1], G[1]]
        three = [False]

        ready_at = [0.0, 0.0, 0.0]

        def step(s):
            Q.newest = None
            try:
                later = next(running[s])
            except StopIteration:
                running[s] = None
                return True
            if Q.newest is not None:
                ready_at[s] = Q.newest + HOP
            if later is not None:
                ready_at[s] = max(ready_at[s], later)
            return Q.newest is not None or later is not None

        def fill():
            for s in range(3):
                if running[s] is None and jobs and (s < 2 or three[0]):
                    running[s] = jobs.popleft()(side[s], W[s], s)
                    ready_at[s] = max([ready_at[s]] + [w.t + HOP for w in side[s].free])

        def advance():
            stuck = set()
            while True:
                fill()
                due = [(ready_at[s], s) for s in range(3) if running[s] is not None and s not in stuck
                       and ready_at[s] <= Q.clock["tensor"]]
                if not due:
                    return
                s = min(due)[1]
                if not step(s):
                    stuck.add(s)

        def tick():
            fill()
            order = sorted((ready_at[s], s) for s in range(3) if running[s] is not None)
            for _, s in order:
                if step(s):
                    return True
            return bool(order)

        def drain():
            while tick():
                pass

        def third_stream(on):
            three[0] = on
            while running[2] is not None:
                tick()

        def when(ops):
            return max([op.t + HOP for op in ops], default=0.0)

        def until(store, key, n=1):
            guard = 0
            while len(store.get(key, ())) < n:
                guard += 1
                assert guard < 5000, key
                tick()
            return store[key]

        def have(store, key, n=1):
            guard = 0
            while len(store.get(key, ())) < n:
                guard += 1
                assert guard < 50000, key
                yield
            yield when(store[key])
            return store[key]

        turn = [0]
        cur = [0]

        def product_block(sh, sl, ready, nready):
            advance()
            if three[0]:
                turn[0] = 0
            pair = G[turn[0] % 2]
            turn[0] += 1
            free = [pair.of_bank(t) for t in range(2)]
            K, _ = WEIGHTS[stream[cur[0]][0]]
            name, _, _, _, width = stream[cur[0]]
            for k0, n in chunks_of(K, width):
                c = cur[0]
                cur[0] += 1
                ensure(c + LA)
                h = c % NH
                for j in range(n):
                    kt = k0 + j
                    ok = until(ready, kt, nready)
                    for t in range(2):
                        o = pair.t[:, 512 * t:512 * t + width]
                        xs = slice(128 * t, 128 * t + 128)
                        ws = slice(j * width, (j + 1) * width)
                        first, last = kt == 0, kt == K // 128 - 1
                        for n3, (l, r) in enumerate(((sh, whi), (sh, wlo), (sl, whi))):
                            w = (hi_op[c], ok, free[t]) if n3 != 1 else (lo_op[c],)
                            op = Q.pe(lambda e: e.matmul(o, l[:, kt, xs], r[h][:, ws], start=first and n3 == 0,
                                                         stop=last and n3 == 2), *w)
                    advance()
                pe_op.append(op)
            return pair, op

        def product_wide(sh, sl, ready, nready):
            third_stream(False)
            turn[0] = 0
            free = [g.free for g in G]
            last = [None, None]
            for i in range(8):
                c = cur[0]
                cur[0] += 1
                ensure(c + LA)
                h, b = c % NH, i % 2
                for j in range(2):
                    kt = i // 2 * 2 + j
                    ok = until(ready, kt, nready)
                    for t in range(2):
                        o = G[b].t[:, 512 * t:512 * t + 512]
                        xs = slice(128 * t, 128 * t + 128)
                        ws = slice(512 * j, 512 * j + 512)
                        for n3, (l, r) in enumerate(((sh, whi), (sh, wlo), (sl, whi))):
                            w = (hi_op[c], ok, free[b]) if n3 != 1 else (lo_op[c],)
                            op = Q.pe(lambda e: e.matmul(o, l[:, kt, xs], r[h][:, ws], start=kt == 0 and n3 == 0,
                                                         stop=kt == 7 and n3 == 2), *w)
                    advance()
                pe_op.append(op)
                last[b] = op
            return [(G[b], last[b]) for b in range(2)]

        def turn_over(src, t, k0, n, dh, dl, ready, waits, gcol=None):
            def job(pair, w, s):
                yield when(waits)
                for i in range(n):
                    op = Q.pe(lambda e, i=i: e.transpose(pair.t[:, 128 * i:128 * i + 128],
                                                         src[:, 128 * i:128 * i + 128], ident),
                              waits, pair.free, ld_cn)
                yield
                ps = pair.t[:, 0:128 * n].rearrange("p (k c) -> p k c", k=n)
                oh = dh[:, k0:k0 + n, 128 * t:128 * t + 128]
                ol = dl[:, k0:k0 + n, 128 * t:128 * t + 128]
                if gcol is not None:
                    tmp = w[0][:, 0:128 * n].rearrange("p (k c) -> p k c", k=n)
                    g = CP[:, gcol + k0:gcol + k0 + n].unsqueeze(2).to_broadcast([128, n, 128])
                    m = Q.dve(lambda e: e.tensor_tensor(tmp, ps, g, ALU.mult), op)
                    hi = Q.act(lambda e: e.activation(oh, tmp, ACT.Copy), m)
                    lo = Q.dve(lambda e: e.tensor_tensor(ol, tmp, oh.bitcast(F), ALU.subtract), hi)
                else:
                    hi = Q.act(lambda e: e.activation(oh, ps, ACT.Copy), op)
                    lo = Q.dve(lambda e: e.tensor_tensor(ol, ps, oh.bitcast(F), ALU.subtract), hi)
                pair.free = [lo]
                for k in range(k0, k0 + n):
                    ready.setdefault(k, []).extend([hi, lo])
                yield
            return job

        def turn_pair(store, p, n, ready):
            def job(pair, w, s):
                src = yield from have(store, ("mx", p), n)
                for t in range(2):
                    for i in range(2):
                        op = Q.pe(lambda e: e.transpose(pair.t[:, 256 * i + 128 * t:256 * i + 128 * t + 128],
                                                        MX[:, t, 256 * p + 128 * i:256 * p + 128 * i + 128], ident),
                                  src, pair.free)
                yield
                ps = pair.t[:, 0:512].rearrange("p (k c) -> p k c", k=2)
                oh, ol = mh[:, 2 * p:2 * p + 2, :], ml[:, 2 * p:2 * p + 2, :]
                hi = Q.act(lambda e: e.activation(oh, ps, ACT.Copy), op)
                lo = Q.dve(lambda e: e.tensor_tensor(ol, ps, oh.bitcast(F), ALU.subtract), hi)
                pair.free = [lo]
                for k in range(2):
                    ready.setdefault(2 * p + k, []).extend([hi, lo])
                yield
            return job

        def rstd_of(ms, eps, scale, *waits):
            n = ms.shape[1]
            y = small(n)
            ln = Q.act(lambda e: e.activation(y, ms, ACT.Ln, scale=scale, bias=consts[:, eps:eps + 1]), c_eps, *waits)
            return y, Q.act(lambda e: e.activation(y, y, ACT.Exp, scale=-0.5), ln)

        junk = GB[:, 1, 0:512]

        class Rms:

            def __init__(self):
                self.ms = [small(2) for _ in range(2)]
                self.ops = [[], []]
                self.r = [None, None]

            def add(self, b, t, dst, *waits):
                op = Q.act(lambda e: e.activation(dst, X[:, t, 512 * b:512 * b + 512], ACT.Square,
                                                  accum_out=self.ms[t][:, b:b + 1]), *waits)
                self.ops[t].append(op)
                if len(self.ops[t]) == 2:
                    s = small(1)
                    m = Q.dve(lambda e: e.tensor_tensor(s, self.ms[t][:, 0:1], self.ms[t][:, 1:2], ALU.add), self.ops[t])
                    self.r[t] = rstd_of(s, 0, 1.0 / D, m)
                return op

        def residual(pair, op, b, alpha, waits=()):
            ops = []
            for t in range(2):
                x = X[:, t, 512 * b:512 * b + 512]
                ops.append(Q.dve(lambda e, t=t, x=x: e.scalar_tensor_tensor(
                    out=x, in0=x, scalar=alpha, in1=pair.t[:, 512 * t:512 * t + 512], op0=ALU.mult, op1=ALU.add),
                    op, waits))
            pair.free = list(ops)
            return ops

        def out_rms(src_h, src_l, ready, nready, gcol):
            nxt, rms = {}, Rms()
            wide = product_wide(src_h, src_l, ready, nready) if src_h is mh else None
            for b in range(2):
                pair, op = wide[b] if wide else product_block(src_h, src_l, ready, nready)
                xs = residual(pair, op, b, 1.0)
                for t in range(2):
                    if gcol is not None:
                        jobs.append(turn_over(X[:, t, 512 * b:512 * b + 512], t, 4 * b, 4, xh, xl, nxt, [xs[t]], gcol))
                    rms.add(b, t, MSQ[t][:, 0:512], xs[t], rms.ops[t])
            return nxt, rms

        gb_use = [[]]

        def load_gb(g, b=None):
            w = gb_use[0]
            op = Q.dma("gpsimd", s_gb, GB[:, 0, :], g.partition_broadcast(128), w)
            if b is not None:
                op = Q.dma("gpsimd", s_gb, GB[:, 1, :], b.partition_broadcast(128), w)
            return op

        def out_ln(src_h, src_l, ready, nready, gb, last=False):
            st = [small(12) for _ in range(2)]
            sts = [[], []]
            wide = product_wide(src_h, src_l, ready, nready) if src_h is mh else None
            for b in range(2):
                pair, op = wide[b] if wide else product_block(src_h, src_l, ready, nready)
                xs = residual(pair, op, b, ALPHA)
                for t in range(2):
                    sts[t].append(Q.dve(lambda e, t=t, b=b: e.bn_stats(st[t][:, 6 * b:6 * b + 6],
                                                                       X[:, t, 512 * b:512 * b + 512]), xs[t]))
            nxt, fin = {}, []
            drain()
            for t in range(2):
                mv = small(2)
                ag = Q.dve(lambda e, t=t, mv=mv: e.bn_aggr(mv, st[t]), sts[t])
                r, ro = rstd_of(mv[:, 1:2], 1, 1.0, ag)
                x = X[:, t, :]
                o = Q.dve(lambda e, x=x, mv=mv: e.scalar_tensor_tensor(
                    out=x, in0=x, scalar=mv[:, 0:1], in1=GB[:, 0, :], op0=ALU.subtract, op1=ALU.mult), ag, gb)
                o = Q.dve(lambda e, x=x, r=r: e.scalar_tensor_tensor(
                    out=x, in0=x, scalar=r, in1=GB[:, 1, :], op0=ALU.mult, op1=ALU.add), o, ro)
                fin.append(o)
                if not last:
                    jobs.append(turn_over(x, t, 0, 8, xh, xl, nxt, [o]))
            gb_use[0] = fin
            return nxt, fin

        def feed_forward(ready, rms):
            done = {}

            def finish(b, width, a_ops, s_, pair, op):
                ops = []
                for t in range(2):
                    h = s_[:, t, 0:width]
                    ps = pair.t[:, 512 * t:512 * t + width]
                    if rms is not None:
                        ops.append(Q.dve(lambda e, h=h, ps=ps, t=t: e.scalar_tensor_tensor(
                            out=h, in0=ps, scalar=rms.r[t][0], in1=h, op0=ALU.mult, op1=ALU.mult), op, a_ops[t]))
                    else:
                        ops.append(Q.dve(lambda e, h=h, ps=ps: e.tensor_tensor(h, ps, h, ALU.mult), op, a_ops[t]))
                pair.free = list(ops)
                for t in range(2):
                    jobs.append(turn_over(s_[:, t, 0:width], t, 4 * b, width // 128, hh, hl, done, [ops[t]]))

            for b, width in enumerate(blocks_of(FF)):
                s_ = sa[b % 2]
                pair, op = product_block(xh, xl, ready, 4)
                if b >= 2:
                    until(done, 4 * (b - 2), 4)
                a_ops = []
                for t in range(2):
                    o, ps = s_[:, t, 0:width], pair.t[:, 512 * t:512 * t + width]
                    sc = rms.r[t][0] if rms is not None else 1.0
                    a_ops.append(Q.act(lambda e, o=o, ps=ps, sc=sc: e.activation(o, ps, ACT.Silu, scale=sc), op,
                                       [rms.r[t][1]] if rms is not None else None,
                                       done[4 * (b - 2)] if b >= 2 else None))
                pair.free = list(a_ops)
                if b == len(blocks_of(FF)) - 1:
                    exp_tables()
                pair, op = product_block(xh, xl, ready, 4)
                finish(b, width, a_ops, s_, pair, op)
            return done

        def softmax4(pair, w, t, qs, ks, mask, scale, nk, stride, waits, mwaits=()):
            for i in range(4):
                at = 512 * (i % 2) + 256 * (i // 2)
                op = Q.pe(lambda e: e.matmul(pair.t[:, at:at + nk], qs[i], ks[i], start=True, stop=True),
                          waits, pair.free)
            yield
            S = w[0][:, 0:4 * stride].rearrange("p (h k) -> p h k", h=4)[:, :, 0:nk]
            mx, sm, rs = small(4), small(4), small(4)
            m = []
            for b in range(2):
                ps = pair.t[:, 512 * b:512 * b + 512].rearrange("p (h k) -> p h k", h=2)[:, :, 0:nk]
                m.append(Q.dve(lambda e: e.scalar_tensor_tensor(
                    out=S[:, b:4:2, :], in0=ps, scalar=scale, in1=mask[:, b:4:2, :],
                    op0=ALU.mult, op1=ALU.add), op, mwaits))
            r = Q.dve(lambda e: e.tensor_reduce(mx, S, X_AX, ALU.max), m)
            ng = Q.dve(lambda e: e.tensor_scalar(mx, mx, -1.0e20, -1.0, ALU.max, ALU.mult), r)
            ex = [Q.act(lambda e, i=i: e.activation(S[:, i, :], S[:, i, :], ACT.Exp, bias=mx[:, i:i + 1],
                                                    accum_out=sm[:, i:i + 1]), ng) for i in range(4)]
            g = Q.dve(lambda e: e.tensor_scalar(sm, sm, 1.0e-30, None, ALU.max), ex)
            rc = Q.dve(lambda e: e.reciprocal(rs, sm), g)
            yield
            return S, rs, ex, rc

        def weigh(pair, w, S, nk, vs, ow, waits, vwaits, n=4):
            nb = (nk + 127) // 128
            kp = min(nk, 128)
            for i in range(n):
                for b in range(nb):
                    at = (i * nb + b) * 128
                    op = Q.pe(lambda e, i=i, b=b, at=at: e.transpose(
                        pair.t[0:kp, at:at + 128], S[:, i, 128 * b:128 * b + kp], ident), waits)
            yield
            half = n * nb * 64
            e1_ = Q.act(lambda e: e.activation(w[1][0:kp, 0:half], pair.t[0:kp, 0:half], ACT.Copy), op)
            wt = e1_ if half < 512 else None
            e2_ = Q.dve(lambda e: e.tensor_copy(w[1][0:kp, half:2 * half], pair.t[0:kp, half:2 * half]), op, wt)
            yield
            for i in range(n):
                for b in range(nb):
                    at = (i * nb + b) * 128
                    op = Q.pe(lambda e, i=i, b=b, at=at: e.matmul(
                        pair.t[:, ow * i:ow * i + ow], w[1][0:kp, at:at + 128], vs[i][b],
                        start=b == 0, stop=b == nb - 1), e1_, e2_, vwaits)
            yield
            return op

        def sigmoid(dst, src, *waits):
            o = Q.dve(lambda e: e.tensor_scalar(dst, src, -1.0, 80.0, ALU.mult, ALU.min), *waits)
            o = Q.act(lambda e: e.activation(dst, dst, ACT.Exp), o)
            o = Q.act(lambda e: e.activation(dst, dst, ACT.Ln, bias=1.0), o)
            return Q.act(lambda e: e.activation(dst, dst, ACT.Exp, scale=-1.0), o)

        def evacuate(pair, op, at, width, rms, over=None):
            ops = []
            for t in range(2):
                o, ps = PJ[:, t, at:at + width], pair.t[:, 512 * t:512 * t + width]
                sc = rms.r[t][0] if rms is not None else 1.0
                w = (op, [rms.r[t][1]] if rms is not None else None, over)
                if t == 0:
                    ops.append(Q.act(lambda e: e.activation(o, ps, ACT.Copy, scale=sc), *w))
                else:
                    ops.append(Q.dve(lambda e: e.tensor_scalar(o, ps, sc, None, ALU.mult), *w))
            pair.free = list(ops)
            return ops

        def rotate(t, at, nh, half, tc, ts, *waits):
            w = 2 * half
            x = PJ[:, t, at:at + nh * w].rearrange("p (h c) -> p h c", h=nh)
            y = MX[:, t, 512:512 + nh * w].rearrange("p (h c) -> p h c", h=nh)
            co = CN[:, tc + w * t:tc + w * t + w].unsqueeze(1).to_broadcast([128, nh, w])
            s0 = CN[:, ts + w * t:ts + w * t + half].unsqueeze(1).to_broadcast([128, nh, half])
            s1 = CN[:, ts + w * t + half:ts + w * t + w].unsqueeze(1).to_broadcast([128, nh, half])
            p = Q.dve(lambda e: e.tensor_tensor(y[:, :, 0:half], x[:, :, half:w], s0, ALU.mult), ld_cn, *waits)
            p = Q.dve(lambda e: e.tensor_tensor(y[:, :, half:w], x[:, :, 0:half], s1, ALU.mult), p)
            q = Q.dve(lambda e: e.tensor_tensor(x, x, co, ALU.mult), p)
            return Q.dve(lambda e: e.tensor_tensor(x, x, y, ALU.add), q)

        rms = Rms()
        nxt = {}
        for t in range(2):
            for b in range(2):
                rms.add(b, t, MSQ[t][:, :], ld_x, rms.ops[t])
                jobs.append(turn_over(X[:, t, 512 * b:512 * b + 512], t, 4 * b, 4, xh, xl, nxt, [ld_x], GM0))
        drain()

        got = {}
        NQ, N5, N6, RQ, RK, RV, RG = 0, 512, 1024, 1304, 1816, 2328, 2840

        def job_qt(t):
            def job(pair, w, s):
                yield when([got["nq"][t]])
                for i in range(4):
                    op = Q.pe(lambda e, i=i: e.transpose(pair.t[:, 128 * i:128 * i + 128],
                                                         PJ[:, t, NQ + 128 * i:NQ + 128 * i + 128], ident),
                              got["nq"][t], pair.free)
                yield
                o = Q.act(lambda e: e.activation(QT[:, :, 128 * t:128 * t + 128],
                                                 pair.t[:, 0:512].rearrange("p (h c) -> p h c", h=4), ACT.Copy), op)
                pair.free = [o]
                got.setdefault("qt", []).append(o)
                yield
            return job

        def twice(ap):
            return ap.unsqueeze(1).to_broadcast([128, 2, 64])

        def job_twice(key, at, dst, i0, shifted):
            def job(pair, w, s):
                d = w[0][:, 0:512].rearrange("p (g t c) -> p g t c", g=2, t=2)
                cp = []
                first = Q.pe(lambda e: e.transpose(pair.t[:, 0:128], ident, ident), ld_cn, pair.free)
                for g in range(2):
                    for t in range(2):
                        dd = d[:, g, t, :].rearrange("p (u c) -> p u c", u=2)
                        cp.append(Q.dve(lambda e, g=g, t=t, dd=dd: e.tensor_copy(
                            dd, twice(PJ[:, t, at + 64 * g:at + 64 * g + 64])), first, got[key][t]))
                yield
                for g in range(2):
                    for t in range(2):
                        op = Q.pe(lambda e, g=g, t=t: e.transpose(
                            pair.t[:, 256 * g + 128 * t:256 * g + 128 * t + 128], d[:, g, t, :], ident), cp)
                yield
                ps = pair.t[:, 0:512].rearrange("p (g c) -> p g c", g=2)
                if shifted:
                    o1 = Q.act(lambda e: e.activation(dst[0:64, i0:i0 + 2, :], ps[0:64], ACT.Copy), op)
                    o2 = Q.act(lambda e: e.activation(dst[64:128, i0:i0 + 2, 0:255], ps[64:128, :, 1:256], ACT.Copy), op)
                    ops = [o1, o2]
                else:
                    ops = [Q.act(lambda e: e.activation(dst[:, i0:i0 + 2, :], ps, ACT.Copy), op)]
                pair.free = ops
                got[f"t{i0}{shifted}"] = ops
                yield
            return job

        def job_compress(kind):
            def job(pair, w, s):
                zr = yield from have(got, f"t{2 * kind}True")
                for m in range(16):
                    z = Z[:, 2 * kind:2 * kind + 2, 2 * m:2 * m + 225:16]
                    wt = w1c[:, kind, 64 * m:64 * m + 64]
                    Q.pe(lambda e, m=m, z=z, wt=wt: e.matmul(
                        pair.t[0:64, 0:30].rearrange("p (g i) -> p g i", g=2), wt, z, start=m == 0, stop=m == 15),
                        zr, ld_e, pair.free)
                for m in range(16):
                    wt = w1c[:, kind, 64 * m:64 * m + 64]
                    pos = CP[:, (POSV if kind else POSK) + m:(POSV if kind else POSK) + m + 1]
                    op = Q.pe(lambda e, m=m, pos=pos, wt=wt: e.matmul(
                        pair.t[0:64, 512:513], wt, pos, start=m == 0, stop=m == 15))
                yield
                x, u, v = w[0][0:64, 0:30], w[0][0:64, 32:62], w[0][0:64, 64:94]
                bias = w[0][0:64, 96:97]
                o = Q.dve(lambda e: e.tensor_copy(bias, pair.t[0:64, 512:513]), op)
                o = Q.dve(lambda e: e.tensor_scalar(x, pair.t[0:64, 0:30], bias, None, ALU.add), o)
                o = Q.dve(lambda e: e.tensor_tensor(u, x, x, ALU.mult), o)
                o = Q.dve(lambda e: e.tensor_tensor(u, u, x, ALU.mult), o)
                o = Q.dve(lambda e: e.scalar_tensor_tensor(out=u, in0=u, scalar=0.044715, in1=x,
                                                           op0=ALU.mult, op1=ALU.add), o)
                k = -2.0 * (2.0 / np.pi) ** 0.5
                o = Q.dve(lambda e: e.tensor_scalar(u, u, float(k), 80.0, ALU.mult, ALU.min), o)
                o = Q.act(lambda e: e.activation(u, u, ACT.Exp), o)
                o = Q.dve(lambda e: e.tensor_scalar(u, u, 1.0, None, ALU.add), o)
                o = Q.dve(lambda e: e.reciprocal(v, u), o)
                o = Q.dve(lambda e: e.tensor_tensor(x, x, v, ALU.mult), o)
                yield
                if kind == 0:
                    op = Q.pe(lambda e: e.matmul(pair.t[:, 0:30], w2c[:, 0:128], x, start=True, stop=True), o)
                    yield
                    o = Q.dve(lambda e: e.tensor_copy(CK[:, 0:30], pair.t[:, 0:30]), op)
                else:
                    for g in range(2):
                        op = Q.pe(lambda e, g=g: e.matmul(pair.t[0:15, 64 * g:64 * g + 64], x[:, 15 * g:15 * g + 15],
                                                          w2c[:, 128:192], start=True, stop=True), o)
                    yield
                    o = Q.dve(lambda e: e.tensor_copy(CK[0:15, 64:192], pair.t[0:15, 0:128]), op)
                pair.free = [o]
                got[f"ck{kind}"] = [o]
                yield
            return job

        gates = small(48)
        acc_n = {}

        def job_nsa(branch, g, t):
            def job(pair, w, s):
                qt = yield from have(got, "qt", 2)
                qs = [QT[64 * (i % 2):64 * (i % 2) + 64, 2 * g + i // 2, 128 * t:128 * t + 128] for i in range(4)]
                if branch == 0:
                    wk = yield from have(got, "ck0")
                    wv = yield from have(got, "ck1")
                    nk, stride = 15, 16
                    ks = [CK[64 * (i % 2):64 * (i % 2) + 64, 15 * g:15 * g + 15] for i in range(4)]
                    mask = CN[:, C_CMP + 16 * t:C_CMP + 16 * t + 15]
                    vs = [[CK[0:15, 64 + 64 * g:128 + 64 * g]] for i in range(4)]
                else:
                    i0 = 0 if branch == 1 else 2
                    wk = yield from have(got, f"t{i0}False")
                    nk = 128 * (t + 1)
                    stride = nk
                    ks = [KT[64 * (i % 2):64 * (i % 2) + 64, i0 + g, 0:nk] for i in range(4)]
                    mask = CN[:, C_CM + 256 - nk:C_CM + 256]
                    va = (N5 + 384 if branch == 1 else N6 + 128) + 64 * g
                    wv = got["b5"] if branch == 1 else got["b6"]
                    vs = [[PJ[:, b, va:va + 64] for b in range(t + 1)] for i in range(4)]
                mask = mask.unsqueeze(1).to_broadcast([128, 4, nk])
                S, rs, ex, rc = yield from softmax4(pair, w, t, qs, ks, mask, 0.125, nk, stride, [qt, wk][0] + list(wk))
                gw = yield from have(got, "gates")
                op = yield from weigh(pair, w, S, nk, vs, 64, ex, list(wv))
                gr = small(4)
                m = Q.dve(lambda e: e.tensor_tensor(gr, rs, gates[:, 24 * t + 8 * branch + 4 * g:24 * t + 8 * branch + 4 * g + 4],
                                                    ALU.mult), rc, gw)
                acc = MX[:, t, 256 * g:256 * g + 256].rearrange("p (h c) -> p h c", h=4)
                ps = pair.t[:, 0:256].rearrange("p (h c) -> p h c", h=4)
                gb = gr.unsqueeze(2).to_broadcast([128, 4, 64])
                prev = acc_n.get((g, t))
                if prev is None:
                    o = Q.dve(lambda e: e.tensor_tensor(acc, ps, gb, ALU.mult), m, op)
                    pair.free = [o]
                else:
                    tmp = w[0][:, 0:256].rearrange("p (h c) -> p h c", h=4)
                    q = Q.dve(lambda e: e.tensor_tensor(tmp, ps, gb, ALU.mult), m, op)
                    o = Q.dve(lambda e: e.tensor_tensor(acc, acc, tmp, ALU.add), q, prev)
                    pair.free = [o]
                acc_n[(g, t)] = o
                got.setdefault(("mx", g), []).append(o)
                yield
            return job

        def job_ret(hp):
            def job(pair, w, s):
                rq = yield from have(got, "rq")
                rk = yield from have(got, "rk")
                for i in range(2):
                    for q in range(2):
                        for t in range(2):
                            at = (RK if q else RQ) + 128 * (2 * hp + i)
                            op = Q.pe(lambda e, i=i, q=q, t=t, at=at: e.transpose(
                                pair.t[:, 512 * i + 256 * q + 128 * t:512 * i + 256 * q + 128 * t + 128],
                                PJ[:, t, at:at + 128], ident), rq, rk, pair.free)
                yield
                o1 = Q.act(lambda e: e.activation(w[0][:, 0:512], pair.t[:, 0:512], ACT.Copy), op)
                o2 = Q.dve(lambda e: e.tensor_copy(w[0][:, 512:1024], pair.t[:, 512:1024]), op)
                yield
                for i in range(2):
                    b = 512 * i
                    Q.pe(lambda e, b=b: e.matmul(pair.t[:, b:b + 256], w[0][:, b + 256:b + 384], w[0][:, b:b + 256],
                                                 start=True, stop=True), o1, o2)
                    op = Q.pe(lambda e, b=b: e.matmul(pair.t[:, b + 256:b + 384], w[0][:, b + 384:b + 512],
                                                      w[0][:, b + 128:b + 256], start=True, stop=True))
                yield
                ms = []
                for i in range(2):
                    b, r = 512 * i, 256 * (2 * hp + i)
                    ms.append(Q.dve(lambda e, b=b, r=r: e.tensor_tensor(
                        w[1][:, b:b + 256], pair.t[:, b:b + 256], LC[:, r:r + 256], ALU.mult), op, ld_ret))
                    ms.append(Q.dve(lambda e, b=b, r=r: e.tensor_tensor(
                        w[1][:, b + 256:b + 384], pair.t[:, b + 256:b + 384], LC[:, r:r + 128], ALU.mult)))
                yield
                rv = yield from have(got, "rv")
                for i in range(2):
                    b, v = 512 * i, RV + 128 * (2 * hp + i)
                    Q.pe(lambda e, b=b, v=v: e.matmul(pair.t[:, b:b + 128], w[1][:, b:b + 128], PJ[:, 0, v:v + 128],
                                                      start=True, stop=True), ms, rv)
                    Q.pe(lambda e, b=b, v=v: e.matmul(pair.t[:, b + 128:b + 256], w[1][:, b + 128:b + 256],
                                                      PJ[:, 0, v:v + 128], start=True, stop=False))
                    op = Q.pe(lambda e, b=b, v=v: e.matmul(pair.t[:, b + 128:b + 256], w[1][:, b + 256:b + 384],
                                                           PJ[:, 1, v:v + 128], start=False, stop=True))
                yield
                rg = yield from have(got, "rg")
                st, mv = small(24), small(8)
                va = small(4)
                ags = []
                for i in range(2):
                    for t in range(2):
                        j = 2 * i + t
                        ps = pair.t[:, 512 * i + 128 * t:512 * i + 128 * t + 128]
                        o = Q.dve(lambda e, j=j, ps=ps: e.bn_stats(st[:, 6 * j:6 * j + 6], ps), op)
                        ags.append(Q.dve(lambda e, j=j: e.bn_aggr(mv[:, 2 * j:2 * j + 2], st[:, 6 * j:6 * j + 6]), o))
                o = Q.dve(lambda e: e.tensor_copy(va, mv[:, 1:8:2]), ags)
                r, ro = rstd_of(va, 1, 1.0, o)
                fin = []
                for i in range(2):
                    for t in range(2):
                        j = 2 * i + t
                        c = 128 * (2 * hp + i)
                        ps = pair.t[:, 512 * i + 128 * t:512 * i + 128 * t + 128]
                        tmp = w[0][:, 128 * j:128 * j + 128]
                        o = Q.dve(lambda e, j=j, ps=ps, tmp=tmp: e.tensor_scalar(
                            tmp, ps, mv[:, 2 * j:2 * j + 1], r[:, j:j + 1], ALU.subtract, ALU.mult), ro)
                        fin.append(Q.dve(lambda e, t=t, c=c, tmp=tmp: e.tensor_tensor(
                            MX[:, t, 512 + c:640 + c], tmp, PJ[:, t, RG + c:RG + c + 128], ALU.mult), o, rg))
                        got.setdefault(("mx", 2 + hp), []).append(fin[-1])
                pair.free = fin
                yield
            return job

        third_stream(True)

        def e_block(key, at, width):
            pair, op = product_block(xh, xl, nxt, 4)
            got[key] = evacuate(pair, op, at, width, rms)

        e_block("nq", NQ, 512)
        jobs.extend([job_qt(0), job_qt(1)])
        e_block("b5", N5, 512)
        jobs.append(job_twice("b5", N5, Z, 0, True))
        jobs.append(job_twice("b5", N5 + 128, Z, 2, True))
        jobs.append(job_twice("b5", N5 + 256, KT, 0, False))
        jobs.extend([job_compress(0), job_compress(1)])
        e_block("b6", N6, 280)
        jobs.append(job_twice("b6", N6, KT, 2, False))
        got["gates"] = [sigmoid(gates[:, 24 * t:24 * t + 24], PJ[:, t, N6 + 256:N6 + 280], got["b6"][t]) for t in range(2)]
        mixed = {}
        for g in range(2):
            for br in (1, 2, 0):
                for t in range(2):
                    jobs.append(job_nsa(br, g, t))
            jobs.append(turn_pair(got, g, 6, mixed))
        e_block("rq_", RQ, 512)
        got["rq"] = [rotate(t, RQ, 4, 64, C_RC, C_RS, got["rq_"][t]) for t in range(2)]
        e_block("rk_", RK, 512)
        got["rk"] = [rotate(t, RK, 4, 64, C_RC, C_RS, got["rk_"][t], got["rq"]) for t in range(2)]
        for hp in range(2):
            jobs.extend([job_ret(hp), turn_pair(got, 2 + hp, 4, mixed)])
        e_block("rv", RV, 512)
        e_block("rg_", RG, 512)
        got["rg"] = []
        for t in range(2):
            rg = PJ[:, t, RG:RG + 512]
            tmp = MSQ[t][:, :]
            o = sigmoid(tmp, rg, got["rg_"][t])
            got["rg"].append(Q.dve(lambda e, rg=rg, tmp=tmp: e.tensor_tensor(rg, rg, tmp, ALU.mult), o))
        nxt, rms = out_rms(mh, ml, mixed, 2, GF0)
        last_ret = got[("mx", 2)] + got[("mx", 3)]
        Q.dma("gpsimd", s_h, LC[:, 0:2176], a["hg"], last_ret)
        hid = feed_forward(nxt, rms)
        nxt, rms = out_rms(hh, hl, hid, 4, GM1)

        ffn_done = rms.ops[0] + rms.ops[1]
        Q.dma("gpsimd", s_h, HN[:, 0:D], a["lbl"].partition_broadcast(128), ffn_done)
        ld_h = Q.dma("gpsimd", s_h, HN[:, D:D + 128], a["hng"].partition_broadcast(128), ffn_done)
        wr = Q.dve(lambda e: e.tensor_copy(Wr[:, :], LC[:, 0:1152]), ld_h)
        lb, lt = HN[:, 0:D], GB[:, 1, :]
        o = Q.dve(lambda e: e.tensor_tensor(lt, lb, lb, ALU.subtract), ld_h)
        o = Q.act(lambda e: e.activation(lt, lt, ACT.Exp), o)
        o = Q.dve(lambda e: e.tensor_tensor(lb, lt, lt, ALU.subtract), o)
        lb_op = Q.dve(lambda e: e.tensor_scalar(lb, lb, 0.0, None, ALU.max), o)
        HW = {"w": wr}
        hgot = {}
        hfree = [[], []]

        def job_forget(u):
            def job(pair, w, s):
                first = Q.pe(lambda e: e.transpose(pair.t[:, 0:128], ident, ident), pair.free)
                prior = hgot.get(("done", u - 2))
                b = 1024 * (u % 3)
                if u >= 2:
                    yield from have(hgot, ("done", u - 2), 4)
                fin = []
                prev = []
                for t in range(2):
                    fq, ff = PJ[:, t, b:b + 256], PJ[:, t, b + 256:b + 512]
                    cols = slice(256 * u, 256 * u + 256)
                    lc = slice(256 * (u % 2), 256 * (u % 2) + 256)
                    L, m, z, y = [w[0][:, 256 * i:256 * i + 256] for i in range(4)]
                    q_ = w[1][:, 256 * t:256 * t + 256]
                    evf = hgot[("qf", u)][t]
                    o = Q.act(lambda e: e.activation(L, ff, ACT.Abs), first, evf, prev)
                    o = Q.act(lambda e: e.activation(L, L, ACT.Exp, scale=-1.0), o)
                    oL = Q.act(lambda e, L=L: e.activation(L, L, ACT.Ln, bias=1.0), o)
                    o = Q.dve(lambda e, m=m, ff=ff: e.tensor_scalar(m, ff, -1.0, 40.0, ALU.mult, ALU.min), first, evf, prev)
                    o = Q.act(lambda e, m=m: e.activation(m, m, ACT.Exp), o)
                    o = Q.dve(lambda e, m=m, cols=cols: e.tensor_tensor(m, m, lb[:, cols], ALU.mult), o, lb_op)
                    o2 = Q.act(lambda e, m=m: e.activation(m, m, ACT.Ln, bias=1.0), o)
                    o = Q.dve(lambda e, z=z, ff=ff, L=L: e.scalar_tensor_tensor(
                        out=z, in0=ff, scalar=0.0, in1=L, op0=ALU.min, op1=ALU.subtract), oL)
                    o = Q.dve(lambda e, z=z, m=m: e.tensor_tensor(z, z, m, ALU.add), o, o2)
                    h_ = Q.act(lambda e: e.activation(lfh[:, t, lc], z, ACT.Copy), o, prior)
                    l_ = Q.dve(lambda e: e.tensor_tensor(lfl[:, t, lc], z, lfh[:, t, lc].bitcast(F), ALU.subtract), h_)
                    o = Q.dve(lambda e, y=y, ff=ff, L=L: e.scalar_tensor_tensor(
                        out=y, in0=ff, scalar=0.0, in1=L, op0=ALU.max, op1=ALU.add), oL)
                    o = Q.act(lambda e, y=y: e.activation(y, y, ACT.Exp, scale=-1.0), o)
                    p = Q.dve(lambda e, m=m, cols=cols: e.tensor_scalar(m, lb[:, cols], -1.0, 1.0, ALU.mult, ALU.add), l_)
                    k_ = Q.dve(lambda e, y=y, m=m, ff=ff: e.tensor_tensor(ff, y, m, ALU.mult), o, p)
                    o = sigmoid(q_, fq, first, evf)
                    sc = 128 ** -0.5
                    qq = Q.dve(lambda e, fq=fq, q_=q_: e.scalar_tensor_tensor(
                        out=fq, in0=fq, scalar=sc, in1=q_, op0=ALU.mult, op1=ALU.mult), o)
                    fin += [l_, k_, qq]
                    prev = [l_, k_]
                    yield
                hgot[("in", u)] = list(fin)
                yield
                yield from have(hgot, ("ig", u), 2)
                for t in range(2):
                    gg = PJ[:, t, b + 768:b + 1024]
                    z = w[1][:, 512 + 256 * t:768 + 256 * t]
                    o = sigmoid(z, gg, first, hgot[("ig", u)][t])
                    ng = HN[:, D:D + 128].unsqueeze(1).to_broadcast([128, 2, 128])
                    o = Q.dve(lambda e, z=z, gg=gg, ng=ng: e.tensor_tensor(
                        gg.rearrange("p (h c) -> p h c", h=2), z.rearrange("p (h c) -> p h c", h=2), ng, ALU.mult),
                        o, ld_h)
                    fin.append(o)
                    hgot.setdefault(("g", u), []).append(o)
                pair.free = fin
                yield
            return job

        def job_heads_turn(u):
            def job(pair, w, s):
                inp = yield from have(hgot, ("in", u), 6)
                for i in range(2):
                    for q in range(2):
                        for t in range(2):
                            at = 1024 * (u % 3) + 256 * q + 128 * i
                            o = pair.t[:, 512 * i + 256 * q + 128 * t:512 * i + 256 * q + 128 * t + 128]
                            op = Q.pe(lambda e: e.transpose(o, PJ[:, t, at:at + 128], ident), inp, pair.free)
                yield
                if u >= 2:
                    yield from have(hgot, ("done", u - 2), 4)
                o1 = Q.act(lambda e: e.activation(HT[u % 2][:, 0:512], pair.t[:, 0:512], ACT.Copy), op)
                o2 = Q.dve(lambda e: e.tensor_copy(HT[u % 2][:, 512:1024], pair.t[:, 512:1024]), op)
                hgot[("t", u)] = pair.free = [o1, o2]
                yield
            return job

        def job_head(h, t):
            def job(pair, w, s):
                u, i = h // 2, h % 2
                ub = 1024 * (u % 3)
                lh = slice(256 * (u % 2) + 128 * i, 256 * (u % 2) + 128 * i + 128)
                hc = slice(128 * h, 128 * h + 128)
                KX = HX[:, 128 * (h % 4):128 * (h % 4) + 128]
                qT = HT[u % 2][:, 512 * i + 128 * t:512 * i + 128 * t + 128]
                kT = HT[u % 2][:, 512 * i + 256 + 128 * t:512 * i + 256 + 128 * t + 128]
                v0, v1 = [PJ[:, tt, ub + 512 + 128 * i:ub + 640 + 128 * i] for tt in range(2)]
                inp = yield from have(hgot, ("in", u), 6)
                for part, l in enumerate((lfh, lfl)):
                    for c0, c1, o0 in ((0, 512, 0), (512, 896, 512), (896 + 128 * t, 1024 + 128 * t, 896)):
                        op = Q.pe(lambda e: e.matmul(pair.t[:, o0:o0 + c1 - c0], l[:, t, lh], Wr[:, c0:c1],
                                                     start=part == 0 and o0 % 512 == 0, stop=part == 1,
                                                     skip_group_check=True), inp, wr, pair.free)
                yield
                cp = yield from have(hgot, ("t", u))
                ex = Q.act(lambda e: e.activation(w[0][:, :], pair.t[:, :], ACT.Exp), op)
                nq = 7 + t
                qo = Q.dve(lambda e: e.tensor_tensor(
                    w[1][:, 0:128 * nq].rearrange("p (l c) -> p l c", c=128),
                    w[0][:, 0:128 * nq].rearrange("p (l c) -> p l c", c=128),
                    qT.unsqueeze(1).to_broadcast([128, nq, 128]), ALU.mult), ex, cp)
                if t == 0:
                    kx = Q.dve(lambda e: e.tensor_tensor(KX, w[0][:, 896:1024], kT, ALU.mult), ex,
                               hgot.get(("x", h - 4)))
                    hgot[("kx", h)] = [kx]
                g7 = w[0][:, 0:896].rearrange("p (l c) -> p l c", c=128)
                ko = Q.dve(lambda e: e.tensor_tensor(g7, g7, kT.unsqueeze(1).to_broadcast([128, 7, 128]), ALU.mult), qo)
                yield
                for l in range(7):
                    Q.pe(lambda e: e.matmul(pair.t[:, 128 * l:128 * l + 128], w[0][:, 128 * l:128 * l + 128],
                                            w[1][:, 128 * l:128 * l + 128], start=True, stop=True), ko)
                op = Q.pe(lambda e: e.matmul(pair.t[:, 896:1024], kT, qT, start=True, stop=True))
                yield
                mo = Q.dve(lambda e: e.tensor_tensor(w[0][:, :], pair.t[:, :], LC[:, 1152:2176], ALU.mult), op)
                AT = w[1][:, 0:128]
                ao = Q.dve(lambda e: e.tensor_reduce(AT, w[0][:, :].rearrange("p (l c) -> p c l", c=128),
                                                     X_AX, ALU.add), mo)
                ig = yield from have(hgot, ("ig", u), 2)
                yield
                if t == 1:
                    kx = yield from have(hgot, ("kx", h))
                    xo = Q.pe(lambda e: e.matmul(pair.t[:, 0:128], KX, w[1][:, 896:1024], start=True, stop=True), mo, kx)
                    hgot[("x", h)] = [xo]
                    axo = Q.act(lambda e: e.activation(w[1][:, 128:256], pair.t[:, 0:128], ACT.Copy), xo)
                op = Q.pe(lambda e: e.matmul(pair.t[:, 512:640], AT, v1 if t else v0, start=True, stop=t == 0), ao, ig)
                yield
                if t == 1:
                    op = Q.pe(lambda e: e.matmul(pair.t[:, 512:640], w[1][:, 128:256], v0, start=False, stop=True), axo)
                    yield
                ms = small(1)
                so = Q.act(lambda e: e.activation(w[1][:, 256:384], pair.t[:, 512:640], ACT.Square, accum_out=ms), op)
                r, ro = rstd_of(ms, 0, 1.0 / 128, so)
                go = yield from have(hgot, ("g", u), 2)
                gs = PJ[:, t, ub + 768 + 128 * i:ub + 896 + 128 * i]
                fo = Q.dve(lambda e: e.scalar_tensor_tensor(
                    out=MX[:, t, hc], in0=pair.t[:, 512:640], scalar=r, in1=gs, op0=ALU.mult, op1=ALU.mult), ro, go)
                pair.free = [fo]
                hgot.setdefault(("mx", u), []).append(fo)
                hgot.setdefault(("done", u), []).append(fo)
                yield
            return job

        def until2(store, key, n):
            while len(store.get(key, ())) < n:
                tick()
            return store[key]

        mixed = {}
        third_stream(True)
        for u in range(4):
            pair, op = product_block(xh, xl, nxt, 4)
            over = until2(hgot, ("done", u - 3), 4) if u >= 3 else None
            hgot[("qf", u)] = evacuate(pair, op, 1024 * (u % 3), 512, rms, over)
            jobs.append(job_forget(u))
            pair, op = product_block(xh, xl, nxt, 4)
            hgot[("ig", u)] = evacuate(pair, op, 1024 * (u % 3) + 512, 512, rms, over)
            jobs.append(job_heads_turn(u))
            for h in (2 * u, 2 * u + 1):
                jobs.extend([job_head(h, 0), job_head(h, 1)])
            jobs.append(turn_pair(hgot, u, 4, mixed))
        gb = load_gb(a["fng"])
        nxt, rms = out_rms(mh, ml, mixed, 2, GF1)
        hid = feed_forward(nxt, rms)
        nxt, rms = out_rms(hh, hl, hid, 4, None)
        drain()
        nxt = {}
        fin = []
        for t in range(2):
            x = X[:, t, :]
            fin.append(Q.dve(lambda e, x=x, t=t: e.scalar_tensor_tensor(
                out=x, in0=x, scalar=rms.r[t][0], in1=GB[:, 0, :], op0=ALU.mult, op1=ALU.mult),
                rms.r[t][1], gb, rms.ops[t]))
            jobs.append(turn_over(x, t, 0, 8, xh, xl, nxt, [fin[t]]))
        gb_use[0] = fin

        Q.dma("gpsimd", s_a, AG[:, 0:128], a["asg"].partition_broadcast(128), fin)
        ld_a = Q.dma("gpsimd", s_a, AG[:, 128:384], a["alam"].partition_broadcast(128), fin)
        lam = small(8)
        los = []
        for i in range(2):
            los.append(Q.dve(lambda e, i=i: e.tensor_tensor(AG[:, 128 + 128 * i:192 + 128 * i], AG[:, 128 + 128 * i:192 + 128 * i],
                                                            AG[:, 192 + 128 * i:256 + 128 * i], ALU.mult), ld_a))
            los.append(Q.dve(lambda e, i=i: e.tensor_reduce(lam[:, i:i + 1], AG[:, 128 + 128 * i:192 + 128 * i],
                                                            X_AX, ALU.add), los[-1]))
        o = Q.act(lambda e: e.activation(lam[:, 2:4], lam[:, 0:2], ACT.Exp), los)
        o = Q.dve(lambda e: e.tensor_tensor(lam[:, 4:5], lam[:, 2:3], lam[:, 3:4], ALU.subtract), o)
        lam_op = Q.dve(lambda e: e.tensor_scalar(lam[:, 5:6], lam[:, 4:5], LAM0, None, ALU.add), o)
        ag_op = Q.dve(lambda e: e.tensor_scalar(AG[:, 0:128], AG[:, 0:128], 1.0 - LAM0, None, ALU.mult), ld_a)

        agot = {}

        def job_turn(key, qat, kat, i0, n, extra):
            def job(pair, w, s):
                yield when(extra)
                for t in range(2):
                    for q in range(2):
                        for i in range(n):
                            at = (kat if q else qat) + 128 * i
                            op = Q.pe(lambda e, q=q, i=i, t=t, at=at: e.transpose(
                                pair.t[:, (q * n + i) * 256 + 128 * t:(q * n + i) * 256 + 128 * t + 128],
                                PJ[:, t, at:at + 128], ident), extra[t], pair.free)
                yield
                half = 256 * n
                o1 = Q.act(lambda e: e.activation(QTa[:, i0:i0 + n, :], pair.t[:, 0:half].rearrange(
                    "p (i c) -> p i c", i=n), ACT.Copy), op)
                o2 = Q.dve(lambda e: e.tensor_copy(KTa[:, i0:i0 + n, :], pair.t[:, half:2 * half].rearrange(
                    "p (i c) -> p i c", i=n)), op)
                pair.free = [o1, o2]
                agot[key] = [o1, o2]
                yield
            return job

        def job_diff(p, t, vat, vkey):
            def job(pair, w, s):
                kq = yield from have(agot, ("qk", p))
                nk = 128 * (t + 1)
                qs = [QTa[64 * (i % 2):64 * (i % 2) + 64, 2 * p + i // 2, 128 * t:128 * t + 128] for i in range(4)]
                ks = [KTa[64 * (i % 2):64 * (i % 2) + 64, 2 * p + i // 2, 0:nk] for i in range(4)]
                mask = CN[:, C_KM + 256 - nk:C_KM + 256].unsqueeze(1).to_broadcast([128, 4, nk])
                S, rs, ex, rc = yield from softmax4(pair, w, t, qs, ks, mask, 0.125, nk, nk, kq)
                rl = small(2)
                lo = Q.dve(lambda e: e.tensor_scalar(rl, rs[:, 1:4:2], lam[:, 5:6], None, ALU.mult), rc, lam_op)
                cs = []
                for i in range(2):
                    d0, d1 = S[:, 2 * i, :], S[:, 2 * i + 1, :]
                    o = Q.dve(lambda e: e.tensor_scalar(d1, d1, rl[:, i:i + 1], None, ALU.mult), lo)
                    cs.append(Q.dve(lambda e: e.scalar_tensor_tensor(
                        out=d0, in0=d0, scalar=rs[:, 2 * i:2 * i + 1], in1=d1, op0=ALU.mult, op1=ALU.subtract), o))
                vo = yield from have(agot, vkey, 2)
                C2 = S[:, 0:4:2, :]
                vs = [[PJ[:, b, vat + 128 * i:vat + 128 * i + 128] for b in range(t + 1)] for i in range(2)]
                op = yield from weigh(pair, w, C2, nk, vs, 128, cs, list(vo), n=2)
                ms = small(2)
                sq = [Q.act(lambda e, i=i: e.activation(w[0][:, 128 * i:128 * i + 128], pair.t[:, 128 * i:128 * i + 128],
                                                        ACT.Square, accum_out=ms[:, i:i + 1]), op) for i in range(2)]
                r, ro = rstd_of(ms, 1, 1.0 / 128, sq)
                fin = []
                for i in range(2):
                    c = 128 * (2 * p + i)
                    fin.append(Q.dve(lambda e, i=i, c=c: e.scalar_tensor_tensor(
                        out=MX[:, t, c:c + 128], in0=pair.t[:, 128 * i:128 * i + 128], scalar=r[:, i:i + 1],
                        in1=AG[:, 0:128], op0=ALU.mult, op1=ALU.mult), ro, ag_op, agot["rot"]))
                agot.setdefault(("mx", p), []).extend(fin)
                pair.free = fin
                yield
            return job

        agot["rot"] = []
        gb = load_gb(a["lng"][0:D], a["lnb"][0:D])

        def rotate_a(t, at, *waits):
            x = PJ[:, t, at:at + 512].rearrange("p (h c) -> p h c", h=8)
            y = MSQ[t][:, :].rearrange("p (h c) -> p h c", h=8)
            co = CN[:, C_AC + 64 * t:C_AC + 64 * t + 64].unsqueeze(1).to_broadcast([128, 8, 64])
            s0 = CN[:, C_AS + 64 * t:C_AS + 64 * t + 32].unsqueeze(1).to_broadcast([128, 8, 32])
            s1 = CN[:, C_AS + 64 * t + 32:C_AS + 64 * t + 64].unsqueeze(1).to_broadcast([128, 8, 32])
            p = Q.dve(lambda e: e.tensor_tensor(y[:, :, 0:32], x[:, :, 32:64], s0, ALU.mult), *waits)
            p = Q.dve(lambda e: e.tensor_tensor(y[:, :, 32:64], x[:, :, 0:32], s1, ALU.mult), p)
            q = Q.dve(lambda e: e.tensor_tensor(x, x, co, ALU.mult), p)
            return Q.dve(lambda e: e.tensor_tensor(x, x, y, ALU.add), q)

        def a_block(at):
            pair, op = product_block(xh, xl, nxt, 4)
            return evacuate(pair, op, at, 512, None)

        def qk_block(p, at, rot):
            ev = a_block(at)
            if rot:
                ev = [rotate_a(t, at, ev[t]) for t in range(2)]
            jobs.append(job_turn(("qk", p), at, at + 256, 2 * p, 2, ev))

        mixed = {}
        third_stream(True)
        for v in range(2):
            b = 1536 * v
            qk_block(2 * v, b, True)
            agot[("v", v)] = a_block(b + 512)
            for t in range(2):
                jobs.append(job_diff(2 * v, t, b + 512, ("v", v)))
            jobs.append(turn_pair(agot, 2 * v, 4, mixed))
            qk_block(2 * v + 1, b + 1024, True)
            for t in range(2):
                jobs.append(job_diff(2 * v + 1, t, b + 768, ("v", v)))
            jobs.append(turn_pair(agot, 2 * v + 1, 4, mixed))

        nxt, _ = out_ln(mh, ml, mixed, 2, gb)
        gb = load_gb(a["lng"][D:2 * D], a["lnb"][D:2 * D])
        hid = feed_forward(nxt, None)
        nxt, fin = out_ln(hh, hl, hid, 4, gb)
        gb = load_gb(a["lng"][2 * D:3 * D], a["lnb"][2 * D:3 * D])

        agot.clear()

        def job_band(p, t, vat, vkey):
            def job(pair, w, s):
                kq = yield from have(agot, ("qk", p))
                nk = 128 * (t + 1)
                qs = [QTa[64 * (i % 2):64 * (i % 2) + 64, 2 * p + i // 2, 128 * t:128 * t + 128] for i in range(4)]
                ks = [KTa[64 * (i % 2):64 * (i % 2) + 64, 2 * p + i // 2, 0:nk] for i in range(4)]
                tb_op = agot[("tb", p)]
                mask = TB[p % 2][:, :].rearrange("p (h k) -> p h k", h=4)[:, :, 256 - nk:256]
                S, rs, ex, rc = yield from softmax4(pair, w, t, qs, ks, mask, 0.125, nk, nk, kq, tb_op)
                agot.setdefault(("used", p), []).extend(ex[-1:])
                vo = yield from have(agot, vkey, 2)
                vs = [[PJ[:, b, vat + 64 * i:vat + 64 * i + 64] for b in range(t + 1)] for i in range(4)]
                op = yield from weigh(pair, w, S, nk, vs, 64, ex, list(vo))
                o = Q.dve(lambda e: e.tensor_tensor(
                    MX[:, t, 256 * p:256 * p + 256].rearrange("p (h c) -> p h c", h=4),
                    pair.t[:, 0:256].rearrange("p (h c) -> p h c", h=4),
                    rs.unsqueeze(2).to_broadcast([128, 4, 64]), ALU.mult), rc, op)
                agot.setdefault(("mx", p), []).append(o)
                pair.free = [o]
                yield
            return job

        km = CN[:, C_KM:C_KM + 256].unsqueeze(1).to_broadcast([128, 4, 256])
        s_tb = [[sem(f"d_tb{i}"), 0] for i in range(2)]

        def load_bias(p, *waits):
            ld = Q.dma("gpsimd", s_tb[p % 2], TB[p % 2][:, :], a["rel"][:, 1024 * p:1024 * p + 1024], *waits)
            tb = TB[p % 2][:, :].rearrange("p (h k) -> p h k", h=4)
            agot[("tb", p)] = [Q.pool(lambda e: e.tensor_tensor(tb, tb, km, ALU.add), ld)]

        load_bias(0, fin)
        load_bias(1, fin)
        mixed = {}
        third_stream(True)
        for v in range(2):
            b = 1536 * v
            if v == 1:
                for p in range(2):
                    load_bias(2 + p, until2(agot, ("used", p), 2))
            qk_block(2 * v, b, False)
            agot[("v", v)] = a_block(b + 512)
            for t in range(2):
                jobs.append(job_band(2 * v, t, b + 512, ("v", v)))
            jobs.append(turn_pair(agot, 2 * v, 2, mixed))
            qk_block(2 * v + 1, b + 1024, False)
            for t in range(2):
                jobs.append(job_band(2 * v + 1, t, b + 768, ("v", v)))
            jobs.append(turn_pair(agot, 2 * v + 1, 2, mixed))
        nxt, _ = out_ln(mh, ml, mixed, 2, gb)
        gb = load_gb(a["lng"][3 * D:4 * D], a["lnb"][3 * D:4 * D])
        hid = feed_forward(nxt, None)
        _, fin = out_ln(hh, hl, hid, 4, gb, last=True)
        drain()
        outs = [Q.dma("sync", s_out, out[128 * t:128 * t + 128, :], X[:, t, :], fin[t]) for t in range(2)]
        assert cur[0] == len(stream)

        Q.count(sems)
        block = ctx.enter_context(nc.Block())

        @block.sync
        def _(e):
            Q.emit("sync", e)
            e.wait_ge(s_out[0], outs[-1].value)

        @block.tensor
        def _(e):
            Q.emit("tensor", e)

        @block.vector
        def _(e):
            Q.emit("vector", e)

        @block.scalar
        def _(e):
            Q.emit("scalar", e)

        @block.gpsimd
        def _(e):
            Q.emit("gpsimd", e)


def kernel(**inputs):
    import concourse.bacc as bacc
    from concourse.bass_utils import run_bass_kernel_spmd

    g = {k: np.asarray(v) for k, v in inputs.items()}
    consts, ret, hg = shape_constants()
    col = lambda v: v.reshape(-1, 128).T
    arrays = {
        "x": g["x"][0],
        "consts": consts, "ret": ret, "hg": hg,
        "cols": np.concatenate([col(g["norm_mix_g"][0]), col(g["norm_ffn_g"][0]), col(g["norm_mix_g"][1]),
                                col(g["norm_ffn_g"][1]), col(g["cmp_pos_k"][0].reshape(-1)),
                                col(g["cmp_pos_v"][0].reshape(-1))], 1),
        "cw1k": g["cmp_w1_k"][0].reshape(16, 128, 64).transpose(1, 0, 2).reshape(128, 1024),
        "cw1v": g["cmp_w1_v"][0].reshape(16, 128, 64).transpose(1, 0, 2).reshape(128, 1024),
        "cw2k": g["cmp_w2_k"][0], "cw2v": g["cmp_w2_v"][0],
        "lbl": g["hgrn_lb_logits"][0], "hng": g["hgrn_norm_g"][0], "fng": g["final_norm_g"],
        "asg": g["a_subln_g_2"][0], "alam": g["a_lambda_2"][0].reshape(-1),
        "lng": g["ln_g_2"].reshape(-1), "lnb": g["ln_b_2"].reshape(-1),
    }
    at = 128 - np.arange(128)[:, None] + np.arange(256)[None, :]
    arrays["rel"] = g["b_rel_bias_2"][0][:, at].transpose(1, 0, 2).reshape(128, 4096)
    ffi, ffo = g["ffn_w_in_2"], g["ffn_w_out_2"]
    qkv_b = np.concatenate([g["b_w_q_2"][0], g["kv_w_2"]], 1)
    mats = {
        "w_e": g["even_w_in"][0][:, E_COLS], "w_eo": g["even_w_out"][0][ranges((512, 512), (0, 512))],
        "w_h": g["odd_w_in"][0][:, H_COLS], "w_ho": g["odd_w_out"][0],
        "w_a": g["a_w_qkv_2"][0][:, A_COLS], "w_ao": g["a_w_o_2"][0],
        "w_b": qkv_b[:, A_COLS], "w_bo": g["b_w_o_2"][0],
    }
    for i in range(2):
        mats[f"g{i}"], mats[f"u{i}"], mats[f"d{i}"] = g["ffn_w1"][i], g["ffn_w3"][i], g["ffn_w2"][i]
        mats[f"g{i + 2}"], mats[f"u{i + 2}"], mats[f"d{i + 2}"] = ffi[i][:, :FF], ffi[i][:, FF:], ffo[i]
    for name, w in mats.items():
        arrays[name] = lay_out(w, name)
    arrays = {k: np.ascontiguousarray(v) for k, v in arrays.items()}

    nc = bacc.Bacc("TRN2", target_bir_lowering=False, num_devices=1)
    aps = {k: nc.dram_tensor(f"in_{k}", v.shape, mybir.dt.from_np(v.dtype), kind="ExternalInput").ap()
           for k, v in arrays.items()}
    out = nc.dram_tensor("out_0", (256, D), F, kind="ExternalOutput").ap()
    program(nc, aps, out)
    r = run_bass_kernel_spmd(nc, [{f"in_{k}": v for k, v in arrays.items()}], core_ids=[0])
    return r.results[0]["out_0"].reshape(1, 256, D)
```
